# Optimizing a Trainium2 kernel written in Bass

```python
import math
import jax, jax.numpy as jnp
from jax import lax
import numpy as np

D_MODEL = 2048
BATCH = 1
SEQ = 256
DEPTH = 2

CHUNK = 64
N_MIXERS = 2
N_ATTN_LAYERS = (DEPTH + 1) // 2
N_SGU_LAYERS = DEPTH // 2

HEAD_DIM = 64
N_HEADS = D_MODEL // HEAD_DIM
N_KV_HEADS = 4
GROUP = N_HEADS // N_KV_HEADS
Q_WIDTH = N_HEADS * HEAD_DIM
KV_WIDTH = N_KV_HEADS * HEAD_DIM
QKV_WIDTH = Q_WIDTH + 2 * KV_WIDTH
WINDOW = 128
WINDOW_CHUNKS = WINDOW // CHUNK
BAND = WINDOW_CHUNKS * CHUNK
ROT_DIM = HEAD_DIM // 4
ROPE_THETA = 500000.0
NEG_INF = -1e30

SGU_BLOCK = 128
SGU_WIDTH = D_MODEL
SGU_GROUPS = 8
SGU_GROUP_DIM = SGU_WIDTH // SGU_GROUPS

D_FF = 4 * D_MODEL

NORM_EPS = 1e-6
POS_OFFSET_MAX = 65536

kernel_name = "hybrid_swa_sink_gmlp_trunk"

def rms_norm(x, g):
    xf = x.astype(jnp.float32)
    y = xf * lax.rsqrt(jnp.mean(xf * xf, axis=-1, keepdims=True) + NORM_EPS)
    return (y * g.astype(jnp.float32)).astype(x.dtype)

def partial_rotary(t, cos, sin):
    half = ROT_DIM // 2
    tr = t[..., :ROT_DIM].astype(jnp.float32)
    t1, t2 = tr[..., :half], tr[..., half:]
    rot = jnp.concatenate([t1 * cos - t2 * sin, t2 * cos + t1 * sin], axis=-1)
    return jnp.concatenate([rot.astype(t.dtype), t[..., ROT_DIM:]], axis=-1)

def chunk_band(t):
    parts = []
    for s in range(WINDOW_CHUNKS - 1, -1, -1):
        if s == 0:
            parts.append(t)
        else:
            pad = [(0, 0), (s, 0)] + [(0, 0)] * (t.ndim - 2)
            parts.append(jnp.pad(t[:, :-s], pad))
    return jnp.concatenate(parts, axis=2)

def sliding_window_sink_attention(h, positions, w_qkv, w_o, sinks):
    B, S, _ = h.shape
    n_chunks = S // CHUNK
    qkv = h @ w_qkv
    q = qkv[..., :Q_WIDTH].reshape(B, S, N_HEADS, HEAD_DIM)
    k = qkv[..., Q_WIDTH:Q_WIDTH + KV_WIDTH].reshape(B, S, N_KV_HEADS, HEAD_DIM)
    v = qkv[..., Q_WIDTH + KV_WIDTH:].reshape(B, S, N_KV_HEADS, HEAD_DIM)

    inv_freq = ROPE_THETA ** (-jnp.arange(0, ROT_DIM, 2, dtype=jnp.float32) / ROT_DIM)
    ang = positions.astype(jnp.float32)[..., None] * inv_freq
    cos = jnp.cos(ang)[:, :, None, :]
    sin = jnp.sin(ang)[:, :, None, :]
    q = partial_rotary(q, cos, sin)
    k = partial_rotary(k, cos, sin)

    q = q.reshape(B, n_chunks, CHUNK, N_KV_HEADS, GROUP, HEAD_DIM).astype(jnp.float32)
    kb = chunk_band(k.reshape(B, n_chunks, CHUNK, N_KV_HEADS, HEAD_DIM)).astype(jnp.float32)
    vb = chunk_band(v.reshape(B, n_chunks, CHUNK, N_KV_HEADS, HEAD_DIM)).astype(jnp.float32)

    shift_j = (WINDOW_CHUNKS - 1) - jnp.arange(BAND) // CHUNK
    valid = jnp.arange(n_chunks)[:, None] >= shift_j[None, :]

    scale = 1.0 / math.sqrt(HEAD_DIM)
    scores = jnp.einsum('bcqkgd,bcjkd->bckgqj', q, kb) * scale
    scores = jnp.where(valid[None, :, None, None, None, :], scores, NEG_INF)
    sink = sinks.astype(jnp.float32).reshape(1, 1, N_KV_HEADS, GROUP, 1, 1)
    m = jnp.maximum(jnp.max(scores, axis=-1, keepdims=True), sink)
    p = jnp.exp(scores - m)
    probs = p / (jnp.sum(p, axis=-1, keepdims=True) + jnp.exp(sink - m))
    o = jnp.einsum('bckgqj,bcjkd->bcqkgd', probs, vb)
    o = o.reshape(B, S, Q_WIDTH).astype(h.dtype)
    return o @ w_o

def chunked_spatial_gating(h, w_in, ln_g, ln_b, w_s, b_s):
    B, S, _ = h.shape
    z = jax.nn.gelu(h @ w_in)
    u, v = z[..., :SGU_WIDTH], z[..., SGU_WIDTH:]
    vf = v.astype(jnp.float32)
    mu = jnp.mean(vf, axis=-1, keepdims=True)
    var = jnp.mean(jnp.square(vf - mu), axis=-1, keepdims=True)
    vn = (vf - mu) * lax.rsqrt(var + NORM_EPS) * ln_g.astype(jnp.float32) + ln_b.astype(jnp.float32)
    vn = vn.reshape(B, S // SGU_BLOCK, SGU_BLOCK, SGU_GROUPS, SGU_GROUP_DIM)
    cidx = jnp.arange(SGU_BLOCK) // CHUNK
    mask = cidx[None, :] <= cidx[:, None]
    ws = jnp.where(mask[None], w_s.astype(jnp.float32), 0.0)
    sv = jnp.einsum('gij,bnjgc->bnigc', ws, vn) + b_s.astype(jnp.float32).T[:, :, None]
    gated = u.astype(jnp.float32) * sv.reshape(B, S, SGU_WIDTH)
    return gated.astype(h.dtype) @ w_out_placeholder_guard(w_s, gated) if False else None

def w_out_placeholder_guard(a, b):
    return a

def sgu_mixer(h, w_in, ln_g, ln_b, w_s, b_s, w_out):
    B, S, _ = h.shape
    z = jax.nn.gelu(h @ w_in)
    u, v = z[..., :SGU_WIDTH], z[..., SGU_WIDTH:]
    vf = v.astype(jnp.float32)
    mu = jnp.mean(vf, axis=-1, keepdims=True)
    var = jnp.mean(jnp.square(vf - mu), axis=-1, keepdims=True)
    vn = (vf - mu) * lax.rsqrt(var + NORM_EPS) * ln_g.astype(jnp.float32) + ln_b.astype(jnp.float32)
    vn = vn.reshape(B, S // SGU_BLOCK, SGU_BLOCK, SGU_GROUPS, SGU_GROUP_DIM)
    cidx = jnp.arange(SGU_BLOCK) // CHUNK
    mask = cidx[None, :] <= cidx[:, None]
    ws = jnp.where(mask[None], w_s.astype(jnp.float32), 0.0)
    sv = jnp.einsum('gij,bnjgc->bnigc', ws, vn) + b_s.astype(jnp.float32).T[:, :, None]
    gated = u.astype(jnp.float32) * sv.reshape(B, S, SGU_WIDTH)
    return gated.astype(h.dtype) @ w_out

def squared_relu_mlp(h, w_up, w_down):
    return jnp.square(jax.nn.relu(h @ w_up)) @ w_down

def setup_inputs(seed: int = 0) -> dict:
    key = jax.random.key(seed)
    ks = jax.random.split(key, 16)
    f32 = jnp.float32
    x = jax.random.normal(ks[0], (BATCH, SEQ, D_MODEL), f32)
    offsets = jax.random.randint(ks[1], (BATCH, 1), 0, POS_OFFSET_MAX, dtype=jnp.int32)
    positions = offsets + jnp.arange(SEQ, dtype=jnp.int32)[None, :]
    norm_gains = 1.0 + 0.05 * jax.random.normal(ks[2], (DEPTH, 4, D_MODEL), f32)
    attn_w_qkv = jax.random.normal(ks[3], (N_ATTN_LAYERS, D_MODEL, QKV_WIDTH), f32) * D_MODEL ** -0.5
    attn_w_o = jax.random.normal(ks[4], (N_ATTN_LAYERS, Q_WIDTH, D_MODEL), f32) * Q_WIDTH ** -0.5
    attn_sinks = jax.random.normal(ks[5], (N_ATTN_LAYERS, N_HEADS), f32)
    sgu_w_in = jax.random.normal(ks[6], (N_SGU_LAYERS, D_MODEL, 2 * SGU_WIDTH), f32) * D_MODEL ** -0.5
    sgu_ln_g = 1.0 + 0.05 * jax.random.normal(ks[7], (N_SGU_LAYERS, SGU_WIDTH), f32)
    sgu_ln_b = 0.02 * jax.random.normal(ks[8], (N_SGU_LAYERS, SGU_WIDTH), f32)
    sgu_w_s = jax.random.normal(ks[9], (N_SGU_LAYERS, SGU_GROUPS, SGU_BLOCK, SGU_BLOCK), f32) * SGU_BLOCK ** -0.5
    sgu_b_s = 0.1 * jax.random.normal(ks[10], (N_SGU_LAYERS, SGU_GROUPS, SGU_BLOCK), f32)
    sgu_w_out = jax.random.normal(ks[11], (N_SGU_LAYERS, SGU_WIDTH, D_MODEL), f32) * SGU_WIDTH ** -0.5
    mlp_w_up = jax.random.normal(ks[12], (DEPTH, D_MODEL, D_FF), f32) * D_MODEL ** -0.5
    mlp_w_down = jax.random.normal(ks[13], (DEPTH, D_FF, D_MODEL), f32) * D_FF ** -0.5
    return {"x": x, "positions": positions, "norm_gains": norm_gains,
            "attn_w_qkv": attn_w_qkv, "attn_w_o": attn_w_o, "attn_sinks": attn_sinks,
            "sgu_w_in": sgu_w_in, "sgu_ln_g": sgu_ln_g, "sgu_ln_b": sgu_ln_b,
            "sgu_w_s": sgu_w_s, "sgu_b_s": sgu_b_s, "sgu_w_out": sgu_w_out,
            "mlp_w_up": mlp_w_up, "mlp_w_down": mlp_w_down}

def reference(x, positions, norm_gains, attn_w_qkv, attn_w_o, attn_sinks,
              sgu_w_in, sgu_ln_g, sgu_ln_b, sgu_w_s, sgu_b_s, sgu_w_out,
              mlp_w_up, mlp_w_down):
    h = x
    for i in range(DEPTH):
        g = norm_gains[i]
        j = i // N_MIXERS
        a = rms_norm(h, g[0])
        if i % N_MIXERS == 0:
            a = sliding_window_sink_attention(a, positions, attn_w_qkv[j], attn_w_o[j], attn_sinks[j])
        else:
            a = sgu_mixer(a, sgu_w_in[j], sgu_ln_g[j], sgu_ln_b[j], sgu_w_s[j], sgu_b_s[j], sgu_w_out[j])
        h = h + rms_norm(a, g[1])
        c = squared_relu_mlp(rms_norm(h, g[2]), mlp_w_up[i], mlp_w_down[i])
        h = h + rms_norm(c, g[3])
    return h


_drawn_inputs = setup_inputs


def setup_inputs(seed=0):
    import zlib

    import numpy as np

    out = dict(_drawn_inputs(seed))
    spreads = {}
    factors = {'attn_sinks': 6.809, 'sgu_ln_b': 5.769}
    for name, (base, spread) in spreads.items():
        noise = np.random.default_rng([zlib.crc32(name.encode()), seed]).standard_normal(out[name].shape)
        drawn = base * np.exp(spread * noise) if base else spread * noise
        out[name] = __import__('jax').numpy.asarray(drawn.astype(out[name].dtype))
    for name, factor in factors.items():
        out[name] = (out[name] * factor).astype(out[name].dtype)
    return out
```

```python
import math
from contextlib import ExitStack, contextmanager

import numpy as np

import concourse.bass as bass
from concourse import mybir

F32 = mybir.dt.float32
F32R = mybir.dt.float32r
I32 = mybir.dt.int32
ALU = mybir.AluOpType
ACT = mybir.ActivationFunctionType
AX_X = mybir.AxisListType.X

P = 128
SEQ = 256
TOK = SEQ // P
D = 2048
KB = D // P
COL = 512
NB = D // COL
SLAB_KB = 2
SLAB = SLAB_KB * COL
SLOTS = 4
PAIRS = KB // SLAB_KB // 2
QUARTERS = 4
HEADS, HD, KVH = 32, 64, 4
GROUP = HEADS // KVH
PAIRED = GROUP // 2
CHUNK = 64
ROT = HD // 4
HALF = ROT // 2
THETA = 500000.0
SG = 8
SGD = D // SG
EPS = 1e-6
SCALE = 1.0 / math.sqrt(HD)
UNITS = D // 256

B_KV, B_Q, B_WO = 0, 1, 5
B_MLP0 = B_WO + NB
B_V = B_MLP0 + 2 * NB * QUARTERS
B_U, B_OUT = B_V + NB, B_V + 2 * NB
B_MLP1 = B_V + 3 * NB
BLOCKS = B_MLP1 + 2 * NB * QUARTERS

T_MLP0 = 2 * UNITS
T_V = T_MLP0 + 2 * NB * QUARTERS
T_U = T_V + UNITS
T_MLP1 = T_U + 2 * NB + UNITS

TWO_PI = 2 * math.pi
PI_1 = 6.28125
PI_2 = float(np.float32(math.floor((TWO_PI - PI_1) * 2.0 ** 19) / 2.0 ** 19))
PI_3 = float(np.float32(TWO_PI - PI_1 - PI_2))
ROUNDER = 1.5 * 2.0 ** 23
PI_MAX = float(np.nextafter(np.float32(math.pi), np.float32(0)))


class Chain:

    def __init__(self, eng, sem):
        self.eng, self.sem, self.n = eng, sem, 0

    def link(self, ins):
        self.n = self.n + 1
        ins.then_inc(self.sem, 1)
        self.eng.wait_ge(self.sem, self.n)

    @contextmanager
    def loop(self, start, end, links):
        before = self.n
        with self.eng.Fori(start, end) as i:
            self.n = (i - start) * links + before
            yield i
        self.n = before + (end - start) * links


def trunk(nc, x, positions, gains, w_qkv, w_o, sinks, w_in, ln_g, ln_b, w_s, b_s, w_out, w_up, w_down, out):
    ctx = ExitStack()
    with ctx:
        def sb(name, shape, dt=F32):
            return ctx.enter_context(nc.sbuf_tensor(name, shape, dt))

        def bank(name):
            return ctx.enter_context(nc.psum_tensor(name, [P, COL], F32))

        def sem(name):
            return ctx.enter_context(nc.semaphore(name))

        h = sb("h", [P, TOK, D])
        y = sb("y", [P, TOK, D])
        a_hi = sb("a_hi", [P, KB, SEQ], F32R)
        a_lo = sb("a_lo", [P, KB, SEQ], F32R)
        b_hi = sb("b_hi", [P, KB, SEQ], F32R)
        b_lo = sb("b_lo", [P, KB, SEQ], F32R)
        w_raw = sb("w_raw", [P, SLOTS, SLAB])
        w_hi = sb("w_hi", [P, SLOTS, SLAB], F32R)
        w_lo = sb("w_lo", [P, SLOTS, SLAB], F32R)
        gain = sb("gain", [P, 2, D])
        s = sb("s", [P, TOK, COL])
        work = sb("work", [P, 3072])
        ws_raw = sb("ws_raw", [P, SG, P])
        junk = sb("junk", [P, COL])
        ident = sb("ident", [P, P])
        gain_rows = sb("gain_rows", [P, P])
        gain_cols = sb("gain_cols", [P, 8 * KB])
        bs_rows = sb("bs_rows", [SG, P])
        bs_cols = sb("bs_cols", [P, SG])
        ssq = sb("ssq", [P, TOK, NB])
        pre_ssq = sb("pre_ssq", [P, TOK])
        mean_sq = sb("mean_sq", [P, TOK])
        root = sb("root", [P, TOK])
        r_in = sb("r_in", [P, TOK])
        r_out = sb("r_out", [P, TOK])
        pos_i = sb("pos_i", [P, TOK], I32)
        pos_f = sb("pos_f", [P, TOK])
        freq = sb("freq", [P, HALF])
        ang = sb("ang", [P, TOK, HALF])
        turns = sb("turns", [P, 2, TOK, HALF])
        red = sb("red", [P, 2, TOK, HALF])
        sincos = sb("sincos", [P, 2, TOK, HALF])
        rot = sb("rot", [P, 4, TOK, GROUP, HALF])
        sink_rows = sb("sink_rows", [P, KVH * 2, 2])
        neg_sink = sb("neg_sink", [P, KVH, 2, 2])
        mx = sb("mx", [P, 2, PAIRED])
        neg_max = sb("neg_max", [P, 2, PAIRED])
        sink_arg = sb("sink_arg", [P, 2, PAIRED])
        sink_exp = sb("sink_exp", [P, 2, PAIRED])
        p_sum = sb("p_sum", [P, 2, PAIRED])
        den = sb("den", [P, 2, PAIRED])
        r_den = sb("r_den", [P, 2, PAIRED])
        stats = sb("stats", [P, TOK, NB, 6])
        moments = sb("moments", [P, TOK, 2])

        yf = y[:, :, :].rearrange("p t n -> p (t n)")
        k_sb = yf[:, 0:1024].rearrange("p (t n) -> p t n", t=TOK)
        kT = yf[:, 1024:2048].rearrange("p (g n) -> p g n", g=KVH)
        qT = yf[:, 2048:3072].rearrange("p (c h n) -> p c h n", c=4, h=PAIRED)
        k_cur = yf[:, 3072:3072 + SEQ]
        probs = work[:, 0:1024].rearrange("p (b n) -> p b n", b=2)
        pT = work[:, 1024:2048].rearrange("p (b n) -> p b n", b=2)
        v_band = work[:, 2048:2816].rearrange("p (v n) -> p v n", v=3)
        v_cur = work[:, 2816:3008].rearrange("p (v n) -> p v n", v=3)
        lnb = work[:, 0:D]
        wsT = work[:, D:D + SG * P].rearrange("p (g n) -> p g n", g=SG)

        acc = [bank("acc0"), bank("acc1")]
        tb = [bank("t0"), bank("t1")]
        scores = ctx.enter_context(nc.psum_tensor("scores", [P, 2, COL], F32))
        sc = [scores[:, 0, :], scores[:, 1, :]]
        ob = [bank("o0"), bank("o1")]

        x_landed = [sem(f"x_landed{i}") for i in range(NB)]
        gains_landed = sem("gains_landed")
        pos_landed = sem("pos_landed")
        sinks_landed = sem("sinks_landed")
        ws_landed = sem("ws_landed")
        row_landed = [sem(f"row_landed{i}") for i in range(6)]
        slab_landed = [sem(f"slab_landed{i}") for i in range(SLOTS)]
        out_stored = sem("out_stored")
        consts_made = sem("consts_made")
        hi_made = sem("hi_made")
        lo_made = sem("lo_made")
        slab_used = sem("slab_used")
        half_done = sem("half_done")
        acc_free = sem("acc_free")
        t_filled = sem("t_filled")
        t_hi = sem("t_hi")
        t_lo = sem("t_lo")
        h_ready = sem("h_ready")
        squared = sem("squared")
        y_squared = sem("y_squared")
        y_scaled = sem("y_scaled")
        norm_sum = sem("norm_sum")
        norm_mean = sem("norm_mean")
        norm_root = sem("norm_root")
        norm_done = sem("norm_done")
        small_filled = sem("small_filled")
        small_copied = sem("small_copied")
        angles_made = sem("angles_made")
        sincos_made = sem("sincos_made")
        qkv_evac = sem("qkv_evac")
        rotated = sem("rotated")
        kt_filled = sem("kt_filled")
        kt_copied = sem("kt_copied")
        qt_filled = sem("qt_filled")
        qt_copied_act = sem("qt_copied_act")
        qt_copied_dve = sem("qt_copied_dve")
        scores_made = sem("scores_made")
        max_made = sem("max_made")
        exp_made = sem("exp_made")
        probs_made = sem("probs_made")
        pt_filled = sem("pt_filled")
        pt_copied = sem("pt_copied")
        o_filled = sem("o_filled")
        o_hi = sem("o_hi")
        o_lo = sem("o_lo")
        ws_masked = sem("ws_masked")
        normed = sem("normed")
        gates_made = sem("gates_made")
        gates_ready = sem("gates_ready")
        gated = sem("gated")
        out_ready = sem("out_ready")
        dve_chain = sem("dve_chain")

        block = ctx.enter_context(nc.Block())

        def at_least(eng, sem_, value):
            if not isinstance(value, int) or value > 0:
                eng.wait_ge(sem_, value)

        def product_done(eng, blk, t):
            if t == 0:
                eng.wait_ge(half_done, blk + 1)
            else:
                eng.wait_ge(slab_used, (blk + 1) * (2 * PAIRS))

        def keys(c):
            return (CHUNK, 0) if c == 0 else (2 * CHUNK, (c - 1) * CHUNK)

        def after_pair(blk, pair):
            return (blk, pair + 1) if pair + 1 < PAIRS else (blk + 1, 0)

        @block.sync
        def _(sp):
            for c in range(NB):
                sp.dma_start(h[:, :, c * COL:(c + 1) * COL],
                             x[0].rearrange("(t p) n -> p t n", p=P)[:, :, c * COL:(c + 1) * COL]
                             ).then_inc(x_landed[c], 16)

            def load_block(blk, w, col, kb0=0):
                rows = w.rearrange("(k p) n -> p k n", p=P)
                for i in range(2 * PAIRS):
                    at_least(sp, lo_made, blk * (2 * PAIRS) + (i + 1 - SLOTS))
                    src = rows[:, bass.ds(kb0 + i * SLAB_KB, SLAB_KB), bass.ds(col, COL)]
                    sp.dma_start(w_raw[:, i % SLOTS, :].rearrange("p (k n) -> p k n", k=SLAB_KB), src
                                 ).then_inc(slab_landed[i % SLOTS], 16)

            def load_mlp(base, layer):
                for q0, q1 in ((0, 1), (1, QUARTERS)):
                    with sp.Fori(q0, q1) as q:
                        with sp.Fori(0, NB) as j:
                            load_block(q * (2 * NB) + j + base, w_up[layer], q * D + j * COL)
                        with sp.Fori(0, NB) as j:
                            load_block(q * (2 * NB) + j + (base + NB), w_down[layer], j * COL, q * KB)

            load_block(B_KV, w_qkv[0], D)
            with sp.Fori(0, NB) as j:
                load_block(j + B_Q, w_qkv[0], j * COL)
            with sp.Fori(0, NB) as j:
                load_block(j + B_WO, w_o[0], j * COL)
            load_mlp(B_MLP0, 0)
            with sp.Fori(0, NB) as j:
                load_block(j + B_V, w_in[0], j * COL + D)
            with sp.Fori(0, NB) as j:
                load_block(j + B_U, w_in[0], j * COL)
            with sp.Fori(0, NB) as j:
                load_block(j + B_OUT, w_out[0], j * COL)
            load_mlp(B_MLP1, 1)
            for c in range(NB):
                sp.wait_ge(out_ready, c + 1)
                sp.dma_start(out[0].rearrange("(t p) n -> p t n", p=P)[:, :, c * COL:(c + 1) * COL],
                             h[:, :, c * COL:(c + 1) * COL]).then_inc(out_stored, 16)
            sp.wait_ge(out_stored, 16 * NB)

        @block.gpsimd
        def _(pool):
            nc.gpsimd.memset(ident[:, :], 0.0).then_inc(consts_made, 1)
            pool.wait_ge(consts_made, 1)
            nc.gpsimd.affine_select(out=ident[:, :], in_=ident[:, :], compare_op=ALU.not_equal, fill=1.0,
                                    base=0, pattern=[[-1, P]], channel_multiplier=1).then_inc(consts_made, 1)
            for i in range(HALF):
                f = float(np.float32(THETA) ** np.float32(-2.0 * i / ROT))
                nc.gpsimd.memset(freq[:, i:i + 1], f).then_inc(consts_made, 1)

            def load_row(n, dst, row):
                pool.dma_start(dst, row.partition_broadcast(P)).then_inc(row_landed[n], 16)

            load_row(0, gain[:, 0, :], gains[0, 1])
            load_row(1, gain[:, 1, :], gains[0, 3])
            pool.dma_start(ws_raw[:, :, :], w_s[0].rearrange("g i j -> i g j")).then_inc(ws_landed, 16)
            pool.dma_start(bs_rows[:, :], b_s[0]).then_inc(ws_landed, 16)
            pool.wait_ge(y_scaled, 2 * NB)
            load_row(2, gain[:, 0, :], ln_g[0])
            load_row(3, lnb, ln_b[0])
            nc.gpsimd.memset(wsT[CHUNK:P, :, 0:CHUNK], 0.0).then_inc(ws_masked, 1)
            pool.wait_ge(y_scaled, 4 * NB)
            load_row(4, gain[:, 1, :], gains[1, 1])
            pool.wait_ge(normed, 2 * NB)
            load_row(5, gain[:, 0, :], gains[1, 3])

        @block.tensor
        def _(pe):
            def multiply(blk, x_hi, x_lo, pair, half):
                if pair == 0:
                    at_least(pe, acc_free, blk * 2 + (half - 1))
                last = None
                for i in (2 * pair, 2 * pair + 1):
                    if half == 0:
                        pe.wait_ge(lo_made, blk * (2 * PAIRS) + (i + 1))
                    for k in range(SLAB_KB):
                        kb = i * SLAB_KB + k
                        tok = slice(half * P, (half + 1) * P)
                        col = slice(k * COL, (k + 1) * COL)
                        w1, w2 = w_hi[:, i % SLOTS, col], w_lo[:, i % SLOTS, col]
                        nc.tensor.matmul(acc[half][:, :], lhsT=x_hi[:, kb, tok], rhs=w1,
                                         start=(kb == 0), stop=False)
                        nc.tensor.matmul(acc[half][:, :], lhsT=x_hi[:, kb, tok], rhs=w2,
                                         start=False, stop=False)
                        last = nc.tensor.matmul(acc[half][:, :], lhsT=x_lo[:, kb, tok], rhs=w1,
                                                start=False, stop=(kb == KB - 1))
                    if half == 1 and i == 2 * pair:
                        last.then_inc(slab_used, 1)
                if half == 1:
                    last.then_inc(slab_used, 1)
                elif pair == PAIRS - 1:
                    last.then_inc(half_done, 1)

            def transpose_s(t, use, ready, count):
                pe.wait_ge(ready, count)
                at_least(pe, t_lo, use - 1)
                for k in range(4):
                    last = nc.tensor.transpose(tb[t][:, k * P:(k + 1) * P], s[:, t, k * P:(k + 1) * P], ident[:, :])
                last.then_inc(t_filled, 1)

            def transpose_unit(u, use0, first_layer=False):
                if first_layer:
                    if u % 2 == 0:
                        pe.wait_ge(x_landed[u // 2], 16)
                else:
                    pe.wait_ge(h_ready, h_base[0] + u + 1)
                at_least(pe, t_lo, use0 + u - 1)
                for k in range(2):
                    for t in range(TOK):
                        at = (k * TOK + t) * P
                        f = (2 * u + k) * P
                        last = nc.tensor.transpose(tb[u % 2][:, at:at + P], h[:, t, f:f + P], ident[:, :])
                last.then_inc(t_filled, 1)

            def first_block(blk, use0, first_layer=False):
                for u in range(4):
                    transpose_unit(u, use0, first_layer)
                for pair in range(PAIRS):
                    if pair in (1, 2):
                        transpose_unit(2 * pair + 2, use0, first_layer)
                        transpose_unit(2 * pair + 3, use0, first_layer)
                    pe.wait_ge(t_lo, use0 + 2 * pair + 2)
                    multiply(blk, a_hi, a_lo, pair, 0)
                    multiply(blk, a_hi, a_lo, pair, 1)
                h_base[0] += 0 if first_layer else UNITS

            h_base = [0]

            def plain_block(blk, x_hi, x_lo, hooks=None):
                for pair in range(PAIRS):
                    for half in range(TOK):
                        multiply(blk, x_hi, x_lo, pair, half)
                        for step in (hooks or {}).get((pair, half), ()):
                            step()

            def transpose_q(g, t):
                pe.wait_ge(rotated, g + 2)
                for hp in range(PAIRED):
                    last = nc.tensor.transpose(tb[t][:, hp * P:(hp + 1) * P], s[:, t, hp * P:(hp + 1) * P],
                                               ident[:, :])
                last.then_inc(qt_filled, 1)

            def score(g, half):
                pe.wait_ge(qt_copied_dve, g + 1)
                pe.wait_ge(qt_copied_act, g + 1)
                for i in range(2):
                    c = 2 * half + i
                    nk, k0 = keys(c)
                    for e in range(2):
                        for a in range(2):
                            row = slice(e * HD, (e + 1) * HD)
                            last = nc.tensor.matmul(scores[:, e, (2 * i + a) * P:(2 * i + a) * P + nk],
                                                    lhsT=qT[row, c, 2 * a:2 * a + 2, :].rearrange("p h n -> p (h n)"),
                                                    rhs=k_cur[row, k0:k0 + nk], start=True, stop=True)
                last.then_inc(scores_made, 1)

            def transpose_p(g, half):
                pe.wait_ge(probs_made, g * 2 + (half + 1))
                for i in (1, 0):
                    nk, _ = keys(2 * half + i)
                    for m in range(PAIRED):
                        last = nc.tensor.transpose(tb[i][0:nk, m * P:(m + 1) * P],
                                                   probs[:, i, m * P:m * P + nk], ident[:, :])
                last.then_inc(pt_filled, 1)

            def weigh_v(g, half):
                pe.wait_ge(pt_copied, g * 2 + (half + 1))
                for i in (1, 0):
                    c = 2 * half + i
                    nk, _ = keys(c)
                    for e in range(2):
                        last = nc.tensor.matmul(ob[i][e * HD:(e + 1) * HD, 0:256], lhsT=v_cur[0:nk, (0, 0, 1, 2)[c], :],
                                                rhs=pT[0:nk, i, e * 256:(e + 1) * 256], start=True, stop=True)
                last.then_inc(o_filled, 1)

            def attend(g, in_o=False):
                hooks = {
                    (0, 0): [lambda: transpose_q(g, 0)],
                    (0, 1): [lambda: transpose_q(g, 1)],
                    (1, 0): [lambda: score(g, 0)],
                    (2, 0): [lambda: transpose_p(g, 0), lambda: score(g, 1)],
                    (2, 1): [lambda: weigh_v(g, 0)],
                }
                if in_o:
                    hooks[2, 1] += [lambda: transpose_p(g, 1), lambda: weigh_v(g, 1),
                                    lambda: pe.wait_ge(o_lo, 2 * KVH)]
                else:
                    hooks[3, 0] = [lambda: transpose_p(g, 1)]
                    hooks[3, 1] = [lambda: weigh_v(g, 1)]
                return hooks

            def mlp(base, layer, use0):
                def up_to_b(q, j, t):
                    use = q * (2 * NB) + j * 2 + (use0 + UNITS + t)
                    transpose_s(t, use, squared, q * (2 * NB) + j * 2 + (2 * NB * QUARTERS * layer + t + 1))

                def both(q, j):
                    return {(0, 0): [lambda: up_to_b(q, j, 0)], (0, 1): [lambda: up_to_b(q, j, 1)]}

                def quarter(q, blk, first):
                    if first:
                        first_block(blk, use0)
                    else:
                        plain_block(blk, a_hi, a_lo)
                    with pe.Fori(1, NB) as j:
                        plain_block(blk + j, a_hi, a_lo, both(q, j - 1))
                    down(q, blk + NB, 0, both(q, NB - 1))
                    with pe.Fori(1, NB) as j:
                        down(q, blk + (NB + j), j, None)

                def down(q, blk, j, hooks):
                    for pair in range(PAIRS):
                        if hooks and pair == PAIRS - 1:
                            pe.wait_ge(t_lo, q * (2 * NB) + (use0 + UNITS + 2 * NB))
                        for half in range(TOK):
                            multiply(blk, b_hi, b_lo, pair, half)
                            for step in (hooks or {}).get((pair, half), ()):
                                step()

                quarter(0, base, True)
                with pe.Fori(1, QUARTERS) as q:
                    quarter(q, q * (2 * NB) + base, False)

            pe.wait_ge(consts_made, 2)
            pe.wait_ge(gains_landed, 16)
            nc.tensor.transpose(sc[0][:, 0:P], gain_rows[:, :], ident[:, :]).then_inc(small_filled, 1)

            first_block(B_KV, 0, first_layer=True)

            def transpose_k(t):
                pe.wait_ge(rotated, 1)
                for g in range(KVH):
                    last = nc.tensor.transpose(tb[t][:, g * P:(g + 1) * P], k_sb[:, t, g * P:(g + 1) * P],
                                               ident[:, :])
                last.then_inc(kt_filled, 1)

            plain_block(B_Q, a_hi, a_lo, {(0, 0): [lambda: transpose_k(0)], (0, 1): [lambda: transpose_k(1)]})
            pe.wait_ge(kt_copied, 2)
            with pe.Fori(0, KVH - 1) as g:
                plain_block(g + (B_Q + 1), a_hi, a_lo, attend(g))
            pe.wait_ge(o_lo, 2 * (KVH - 1))
            plain_block(B_WO, b_hi, b_lo, attend(KVH - 1, in_o=True))
            with pe.Fori(1, NB) as j:
                plain_block(j + B_WO, b_hi, b_lo)
            mlp(B_MLP0, 0, UNITS)

            first_block(B_V, T_V)
            with pe.Fori(1, NB) as j:
                plain_block(j + B_V, a_hi, a_lo)

            def transpose_ws():
                pe.wait_ge(ws_landed, 32)
                for g in range(SG):
                    last = nc.tensor.transpose(sc[g // 4][:, (g % 4) * P:(g % 4 + 1) * P], ws_raw[:, g, :],
                                               ident[:, :])
                last.then_inc(small_filled, 1)
                nc.tensor.transpose(ob[0][:, 0:SG], bs_rows[:, :], ident[0:SG, 0:SG]).then_inc(small_filled, 1)

            def gate(c):
                for t in range(TOK):
                    pe.wait_ge(normed, 2 * c + t + 1)
                    at_least(pe, gates_ready, 2 * (c - 1) + t + 1)
                    for i in range(2):
                        g = 2 * c + i
                        last = nc.tensor.matmul(sc[t][:, i * SGD:(i + 1) * SGD], lhsT=wsT[:, g, :],
                                                rhs=y[:, t, g * SGD:(g + 1) * SGD], start=True, stop=True)
                    last.then_inc(gates_made, 1)

            def first_gates():
                pe.wait_ge(small_copied, 4)
                pe.wait_ge(ws_masked, 1)
                gate(0)

            plain_block(B_U, a_hi, a_lo, {
                (0, 0): [transpose_ws], (1, 0): [first_gates], (2, 0): [lambda: gate(1)],
                (3, 0): [lambda: gate(2)], (3, 1): [lambda: gate(3)]})

            def u_to_b(j, t):
                transpose_s(t, j * 2 + (T_U + t), gated, j * 2 + (t + 1))

            with pe.Fori(1, NB) as j:
                plain_block(j + B_U, a_hi, a_lo, {(0, 0): [lambda: u_to_b(j - 1, 0)],
                                                  (0, 1): [lambda: u_to_b(j - 1, 1)]})
            def gated_ready():
                pe.wait_ge(t_lo, T_U + 2 * NB)
            plain_block(B_OUT, b_hi, b_lo, {(0, 0): [lambda: u_to_b(NB - 1, 0)],
                                            (0, 1): [lambda: u_to_b(NB - 1, 1)],
                                            (2, 1): [gated_ready]})
            with pe.Fori(1, NB) as j:
                plain_block(j + B_OUT, b_hi, b_lo)
            mlp(B_MLP1, 1, T_MLP1 - UNITS)

        @block.scalar
        def _(act):
            def split_slabs(blk, pair):
                for i in (2 * pair, 2 * pair + 1):
                    act.wait_ge(slab_landed[i % SLOTS], blk * (32 * PAIRS // SLOTS) + 16 * (i // SLOTS + 1))
                    at_least(act, slab_used, blk * (2 * PAIRS) + (i + 1 - SLOTS))
                    nc.scalar.activation(w_hi[:, i % SLOTS, :], w_raw[:, i % SLOTS, :], ACT.Copy).then_inc(hi_made, 1)

            def split_ahead(blk, pair):
                if not (isinstance(blk, int) and blk == BLOCKS - 1 and pair == PAIRS - 1):
                    split_slabs(*after_pair(blk, pair))

            def split_unit(u, use0, norm):
                act.wait_ge(t_filled, use0 + u + 1)
                for k in range(2):
                    kb = 2 * u + k
                    at = k * SEQ
                    last = nc.scalar.activation(a_hi[:, kb, :], tb[u % 2][:, at:at + SEQ], ACT.Copy,
                                                scale=gain_cols[:, norm * KB + kb:norm * KB + kb + 1])
                last.then_inc(t_hi, 1)

            def split_s(t, use, kb0):
                act.wait_ge(t_filled, use + 1)
                nc.scalar.activation(b_hi[:, bass.ds(kb0, 4), t * P:(t + 1) * P],
                                     tb[t][:, :].rearrange("p (k n) -> p k n", k=4), ACT.Copy).then_inc(t_hi, 1)

            def take_root():
                norms[0] += 1
                act.wait_ge(norm_mean, norms[0])
                nc.scalar.activation(root[:, :], mean_sq[:, :], ACT.Sqrt).then_inc(norm_root, 1)

            norms = [0]

            def first_block(blk, use0, norm, layer0=False):
                for u in range(4):
                    split_unit(u, use0, norm)
                for pair in range(PAIRS):
                    split_ahead(blk, pair)
                    if pair < 2:
                        split_unit(2 * pair + 4, use0, norm)
                        split_unit(2 * pair + 5, use0, norm)
                    if pair in (1, 2):
                        t = pair - 1
                        if layer0:
                            for c in range(NB):
                                act.wait_ge(x_landed[c], 16)
                        elif t == 0:
                            h_seen[0] += UNITS
                            act.wait_ge(h_ready, h_seen[0])
                        nc.scalar.activation(
                            b_hi[:, t * 8:(t + 1) * 8, :].rearrange("p k n -> p (k n)"), h[:, t, :],
                            ACT.Square, accum_out=pre_ssq[:, t:t + 1]).then_inc(norm_sum, 1)
                    if pair == 2:
                        take_root()

            h_seen = [0]

            def read_out(blk, t, dst, func):
                product_done(act, blk, t)
                return nc.scalar.activation(dst, acc[t][:, :], func, scale=r_in[:, t:t + 1])

            def square_y(blk, j, t, n):
                act.wait_ge(acc_free, blk * 2 + (t + 1))
                at_least(act, y_squared, j * TOK + (n + t))
                nc.scalar.activation(junk[:, :], y[:, t, bass.ds(j * COL, COL)], ACT.Square,
                                     accum_out=ssq[:, t, bass.ds(j, 1)]).then_inc(y_squared, 1)

            def product_to_y(base, j, n=None):
                for pair in range(PAIRS):
                    split_ahead(base + j, pair)
                if n is not None:
                    for t in range(TOK):
                        square_y(base + j, j, t, n)

            def mlp(base, layer, use0, n):
                sq0 = 2 * NB * QUARTERS * layer

                def up_evac(q, blk, j):
                    for t in range(TOK):
                        n = q * (2 * NB) + j * 2 + (sq0 + t + 1)
                        read_out(blk, t, s[:, t, :], ACT.Relu).then_inc(acc_free, 1)
                        act.wait_ge(acc_free, blk * 2 + (t + 1))
                        nc.scalar.activation(s[:, t, :], s[:, t, :], ACT.Square).then_inc(squared, 1)

                def up_splits(q, j):
                    for t in range(TOK):
                        split_s(t, q * (2 * NB) + j * 2 + (use0 + UNITS + t), j * 4)

                def quarter(q, blk, first, last):
                    if first:
                        first_block(blk, use0, 4 * layer + 2)
                    else:
                        for pair in range(PAIRS):
                            split_ahead(blk, pair)
                    if first:
                        act.wait_ge(norm_done, norms[0])
                    up_evac(q, blk, 0)
                    with act.Fori(1, NB) as j:
                        split_ahead(blk + j, 0)
                        up_splits(q, j - 1)
                        for pair in range(1, PAIRS):
                            split_ahead(blk + j, pair)
                        up_evac(q, blk + j, j)
                    split_ahead(blk + NB, 0)
                    up_splits(q, NB - 1)
                    for pair in range(1, PAIRS):
                        split_ahead(blk + NB, pair)
                    if last:
                        for t in range(TOK):
                            square_y(blk + NB, 0, t, n)
                    if last:
                        with act.Fori(1, NB - 1) as j:
                            product_to_y(blk + NB, j, n)
                        product_to_y(blk + NB, NB - 1, n)
                    else:
                        with act.Fori(1, NB) as j:
                            product_to_y(blk + NB, j)

                quarter(0, base, True, False)
                with act.Fori(1, QUARTERS - 1) as q:
                    quarter(q, q * (2 * NB) + base, False, False)
                quarter(QUARTERS - 1, base + (QUARTERS - 1) * 2 * NB, False, True)

            act.dma_start(gain_rows[:, :], gains.rearrange("l i (k p) -> (l i k) p", p=P)).then_inc(gains_landed, 16)
            act.dma_start(pos_i[:, :], positions[0].rearrange("(t p) -> p t", p=P),
                          allow_slow_non_contiguous=True).then_inc(pos_landed, 16)
            for i in range(2):
                act.dma_start(sink_rows[i * CHUNK:(i + 1) * CHUNK, :, :],
                              sinks[0].rearrange("(a i e) -> i a e", i=2, e=2)[i].partition_broadcast(CHUNK),
                              allow_slow_non_contiguous=True).then_inc(sinks_landed, 16)
            act.wait_ge(small_filled, 1)
            nc.scalar.activation(gain_cols[:, :], sc[0][:, 0:P], ACT.Copy).then_inc(small_copied, 1)
            act.wait_ge(small_copied, 1)
            act.wait_ge(angles_made, 1)
            nc.scalar.activation(sincos[:, :, :, :], red[:, :, :, :], ACT.Sin).then_inc(sincos_made, 1)

            split_slabs(0, 0)
            first_block(B_KV, 0, 0, layer0=True)
            act.wait_ge(norm_done, norms[0])
            for t in range(TOK):
                product_done(act, B_KV, t)
                once = acc[t][:, 0:256].rearrange("p (g d) -> p g d", g=KVH)
                nc.scalar.activation(k_sb[:, t, :].rearrange("p (g e d) -> p g e d", g=KVH, e=2),
                                     once.unsqueeze(2).to_broadcast([P, KVH, 2, HD]), ACT.Copy,
                                     scale=r_in[:, t:t + 1]).then_inc(qkv_evac, 1)
                nc.scalar.activation(v_band[:, 2 * t, :], acc[t][:, 256:512], ACT.Copy, scale=r_in[:, t:t + 1]
                                     ).then_inc(acc_free, 1)

            def q_evac(blk, t):
                read_out(blk, t, s[:, t, :], ACT.Copy).then_inc(acc_free, 1)

            split_ahead(B_Q, 0)
            for t in range(TOK):
                act.wait_ge(kt_filled, t + 1)
                nc.scalar.activation(kT[:, :, t * P:(t + 1) * P],
                                     tb[t][:, :].rearrange("p (g n) -> p g n", g=KVH), ACT.Copy
                                     ).then_inc(kt_copied, 1)
            for pair in range(1, PAIRS):
                split_ahead(B_Q, pair)
            for t in range(TOK):
                q_evac(B_Q, t)

            def copy_qT(g):
                act.wait_ge(qt_filled, g * 2 + 1)
                nc.scalar.activation(qT[:, 0:2, :, :].rearrange("p c h n -> p h c n"),
                                     tb[0][:, :].rearrange("p (h c n) -> p h c n", h=PAIRED, c=2), ACT.Copy
                                     ).then_inc(qt_copied_act, 1)

            def exponentials(g, half):
                act.wait_ge(max_made, g * 2 + (half + 1))
                for i in range(2):
                    nk, _ = keys(2 * half + i)
                    for m in range(PAIRED):
                        e, a = m // 2, m % 2
                        nc.scalar.activation(probs[:, i, m * P:m * P + nk],
                                             scores[:, e, (2 * i + a) * P:(2 * i + a) * P + nk], ACT.Exp,
                                             bias=neg_max[:, i, m:m + 1], scale=SCALE,
                                             accum_out=p_sum[:, i, m:m + 1])
                nc.scalar.activation(sink_exp[:, :, :], sink_arg[:, :, :], ACT.Exp).then_inc(exp_made, 1)

            def copy_pT(g, half):
                act.wait_ge(pt_filled, g * 2 + (half + 1))
                for i in range(2):
                    nk, _ = keys(2 * half + i)
                    last = nc.scalar.activation(pT[0:nk, i, :], tb[i][0:nk, :], ACT.Copy)
                last.then_inc(pt_copied, 1)

            def split_o(g, half):
                act.wait_ge(o_filled, g * 2 + (half + 1))
                for i in range(2):
                    c = 2 * half + i
                    last = nc.scalar.activation(b_hi[:, bass.ds(g * PAIRED, PAIRED), c * CHUNK:(c + 1) * CHUNK],
                                                ob[i][:, 0:256].rearrange("p (h n) -> p h n", h=PAIRED), ACT.Copy)
                last.then_inc(o_hi, 1)

            def attend(blk, g, evac):
                split_ahead(blk, 0)
                copy_qT(g)
                split_ahead(blk, 1)
                exponentials(g, 0)
                split_ahead(blk, 2)
                copy_pT(g, 0)
                exponentials(g, 1)
                split_o(g, 0)
                if evac:
                    split_ahead(blk, 3)
                copy_pT(g, 1)
                if evac:
                    q_evac(blk, 0)
                    q_evac(blk, 1)
                split_o(g, 1)
                if not evac:
                    split_ahead(blk, 3)

            with act.Fori(0, KVH - 1) as g:
                attend(g + (B_Q + 1), g, True)
            attend(B_WO, KVH - 1, False)
            for t in range(TOK):
                square_y(B_WO, 0, t, 0)
            with act.Fori(1, NB) as j:
                product_to_y(B_WO, j, 0)
            take_root()
            mlp(B_MLP0, 0, UNITS, 2 * NB)
            take_root()

            first_block(B_V, T_V, 4)
            act.wait_ge(norm_done, norms[0])

            def v_evac(j):
                for t in range(TOK):
                    read_out(j + B_V, t, y[:, t, bass.ds(j * COL, COL)], ACT.Gelu_apprx_tanh).then_inc(acc_free, 1)

            v_evac(0)
            with act.Fori(1, NB) as j:
                for pair in range(PAIRS):
                    split_ahead(j + B_V, pair)
                v_evac(j)

            def u_evac(j):
                for t in range(TOK):
                    read_out(j + B_U, t, s[:, t, :], ACT.Gelu_apprx_tanh).then_inc(acc_free, 1)

            split_ahead(B_U, 0)
            take_root()
            act.wait_ge(small_filled, 2)
            for i in range(2):
                full = sc[i][:, :].rearrange("p (g n) -> p g n", g=4)
                nc.scalar.activation(wsT[0:CHUNK, 4 * i:4 * i + 4, :], full[0:CHUNK], ACT.Copy)
                nc.scalar.activation(wsT[CHUNK:P, 4 * i:4 * i + 4, CHUNK:P], full[CHUNK:P, :, CHUNK:P],
                                     ACT.Copy).then_inc(small_copied, 1)
            act.wait_ge(small_filled, 3)
            nc.scalar.activation(bs_cols[:, :], ob[0][:, 0:SG], ACT.Copy).then_inc(small_copied, 1)
            for pair in range(1, PAIRS):
                split_ahead(B_U, pair)
            u_evac(0)
            with act.Fori(1, NB) as j:
                split_ahead(j + B_U, 0)
                for t in range(TOK):
                    split_s(t, (j - 1) * 2 + (T_U + t), (j - 1) * 4)
                for pair in range(1, PAIRS):
                    split_ahead(j + B_U, pair)
                u_evac(j)
            split_ahead(B_OUT, 0)
            for t in range(TOK):
                split_s(t, 2 * (NB - 1) + T_U + t, 4 * (NB - 1))
            for pair in range(1, PAIRS):
                split_ahead(B_OUT, pair)
            for t in range(TOK):
                square_y(B_OUT, 0, t, 4 * NB)
            with act.Fori(1, NB) as j:
                product_to_y(B_OUT, j, 4 * NB)
            take_root()
            mlp(B_MLP1, 1, T_MLP1 - UNITS, 6 * NB)
            take_root()

        @block.vector
        def _(dve):
            chain = Chain(dve, dve_chain)
            link = chain.link
            norms, sums, squares, seen_h = [0], [0], [0], [0]

            def split_slabs(blk, pair):
                for i in (2 * pair, 2 * pair + 1):
                    dve.wait_ge(hi_made, blk * (2 * PAIRS) + (i + 1))
                    nc.vector.tensor_tensor(w_lo[:, i % SLOTS, :], w_raw[:, i % SLOTS, :],
                                            w_hi[:, i % SLOTS, :].bitcast(F32), ALU.subtract).then_inc(lo_made, 1)

            def split_ahead(blk, pair):
                if not (isinstance(blk, int) and blk == BLOCKS - 1 and pair == PAIRS - 1):
                    split_slabs(*after_pair(blk, pair))

            def split_unit(u, use0, norm):
                dve.wait_ge(t_hi, use0 + u + 1)
                for k in range(2):
                    kb = 2 * u + k
                    last = nc.vector.scalar_tensor_tensor(
                        out=a_lo[:, kb, :], in0=tb[u % 2][:, k * SEQ:(k + 1) * SEQ],
                        scalar=gain_cols[:, norm * KB + kb:norm * KB + kb + 1],
                        in1=a_hi[:, kb, :].bitcast(F32), op0=ALU.mult, op1=ALU.subtract)
                last.then_inc(t_lo, 1)

            def split_s(t, use, kb0):
                dve.wait_ge(t_hi, use + 1)
                at = (slice(None), bass.ds(kb0, 4), slice(t * P, (t + 1) * P))
                nc.vector.tensor_tensor(b_lo[at], tb[t][:, :].rearrange("p (k n) -> p k n", k=4),
                                        b_hi[at].bitcast(F32), ALU.subtract).then_inc(t_lo, 1)

            def update_h(u):
                f = slice(u * 256, (u + 1) * 256)
                for t in range(TOK):
                    last = nc.vector.scalar_tensor_tensor(out=h[:, t, f], in0=y[:, t, f], scalar=r_out[:, t:t + 1],
                                                          in1=h[:, t, f], op0=ALU.mult, op1=ALU.add)
                last.then_inc(h_ready, 1)

            def mean(sum_):
                norms[0] += 1
                nc.vector.tensor_scalar(mean_sq[:, :], sum_, 1.0 / D, EPS, ALU.mult, ALU.add).then_inc(norm_mean, 1)

            def inverse(dst):
                dve.wait_ge(norm_root, norms[0])
                nc.vector.reciprocal(dst, root[:, :]).then_inc(norm_done, 1)

            def first_block(blk, use0, norm, layer0=False):
                if not layer0:
                    dve.wait_ge(norm_done, norms[0])
                    update_h(0)
                    update_h(1)
                for u in range(4):
                    if not layer0:
                        update_h(u + 2)
                    split_unit(u, use0, norm)
                for pair in range(PAIRS):
                    split_ahead(blk, pair)
                    if pair == 0 and not layer0:
                        update_h(6)
                        update_h(7)
                    if pair < 2:
                        split_unit(2 * pair + 4, use0, norm)
                        split_unit(2 * pair + 5, use0, norm)
                    if pair == 2:
                        sums[0] += TOK
                        dve.wait_ge(norm_sum, sums[0])
                        mean(pre_ssq[:, :])
                        inverse(r_in[:, :])

            def to_y(blk, j, add):
                for t in range(TOK):
                    dst = y[:, t, bass.ds(j * COL, COL)]
                    product_done(dve, blk, t)
                    if add:
                        nc.vector.tensor_tensor(dst, acc[t][:, :], dst, ALU.add).then_inc(acc_free, 1)
                    else:
                        nc.vector.tensor_copy(dst, acc[t][:, :]).then_inc(acc_free, 1)

            def scale_y(j, t, row, n):
                dst = y[:, t, bass.ds(j * COL, COL)]
                dve.wait_ge(y_squared, j * TOK + (n + t + 1))
                nc.vector.tensor_tensor(dst, dst, gain[:, row, bass.ds(j * COL, COL)], ALU.mult).then_inc(y_scaled, 1)

            def product_to_y(blk0, j, add, row, n):
                for pair in range(PAIRS):
                    split_ahead(blk0 + j, pair)
                to_y(blk0 + j, j, add)
                if row is not None:
                    for t in range(TOK):
                        scale_y(j, t, row, n)

            def finish_y(blk0, add, row, n):
                with dve.Fori(1, NB - 1) as j:
                    product_to_y(blk0, j, add, row, n)
                for pair in range(PAIRS):
                    split_ahead(blk0 + NB - 1, pair)
                to_y(blk0 + NB - 1, NB - 1, add)
                scale_y(NB - 1, 0, row, n)
                dve.wait_ge(y_squared, n + 2 * NB)
                link(nc.vector.tensor_reduce(pre_ssq[:, :], ssq[:, :, :], AX_X, ALU.add))
                mean(pre_ssq[:, :])
                scale_y(NB - 1, 1, row, n)
                inverse(r_out[:, :])
                dve.wait_ge(y_scaled, n + 2 * NB)

            def mlp(base, layer, use0, row, n):
                def up_splits(q, j):
                    for t in range(TOK):
                        split_s(t, q * (2 * NB) + j * 2 + (use0 + UNITS + t), j * 4)

                def quarter(q, blk, first, last):
                    if first:
                        first_block(blk, use0, 4 * layer + 2)
                    else:
                        for pair in range(PAIRS):
                            split_ahead(blk, pair)
                    with dve.Fori(1, NB) as j:
                        split_ahead(blk + j, 0)
                        up_splits(q, j - 1)
                        for pair in range(1, PAIRS):
                            split_ahead(blk + j, pair)
                    split_ahead(blk + NB, 0)
                    up_splits(q, NB - 1)
                    for pair in range(1, PAIRS):
                        split_ahead(blk + NB, pair)
                    to_y(blk + NB, 0, not first)
                    if last:
                        for t in range(TOK):
                            scale_y(0, t, row, n)
                        finish_y(blk + NB, True, row, n)
                    else:
                        with dve.Fori(1, NB) as j:
                            product_to_y(blk + NB, j, not first, None, 0)

                quarter(0, base, True, False)
                with dve.Fori(1, QUARTERS - 1) as q:
                    quarter(q, q * (2 * NB) + base, False, False)
                dve.wait_ge(row_landed[1 if layer == 0 else 5], 16)
                quarter(QUARTERS - 1, base + (QUARTERS - 1) * 2 * NB, False, True)

            dve.wait_ge(pos_landed, 16)
            dve.wait_ge(consts_made, 2 + HALF)
            link(nc.vector.tensor_copy(pos_f[:, :], pos_i[:, :]))
            for t in range(TOK):
                last = nc.vector.tensor_scalar(ang[:, t, :], freq[:, :], pos_f[:, t:t + 1], None, ALU.mult)
            link(last)
            for i in range(2):
                last = nc.vector.tensor_scalar(turns[:, i], ang[:, :, :], 1.0 / TWO_PI, 0.25 * i, ALU.mult, ALU.add)
            link(last)
            link(nc.vector.tensor_scalar(turns[:, :, :, :], turns[:, :, :, :], ROUNDER, None, ALU.add))
            link(nc.vector.tensor_scalar(turns[:, :, :, :], turns[:, :, :, :], ROUNDER, None, ALU.subtract))
            for n, part in enumerate((PI_1, PI_2, PI_3)):
                for i in range(2):
                    last = nc.vector.scalar_tensor_tensor(
                        out=red[:, i], in0=turns[:, i], scalar=-part, in1=ang[:, :, :] if n == 0 else red[:, i],
                        op0=ALU.mult, op1=ALU.add)
                link(last)
            link(nc.vector.tensor_scalar(red[:, 1], red[:, 1], math.pi / 2, None, ALU.add))
            nc.vector.tensor_scalar(red[:, :, :, :], red[:, :, :, :], PI_MAX, -PI_MAX, ALU.min, ALU.max
                                    ).then_inc(angles_made, 1)
            dve.wait_ge(sinks_landed, 32)
            link(nc.vector.tensor_scalar(neg_sink[:, :, :, :], sink_rows[:, :, :].rearrange("p (g a) e -> p g e a", a=2),
                                         -1.0, None, ALU.mult))
            dve.wait_ge(small_copied, 1)

            split_slabs(0, 0)
            first_block(B_KV, 0, 0, layer0=True)

            def rotate(x, heads):
                t1, t2 = x[:, :, :, 0:HALF], x[:, :, :, HALF:ROT]
                sin, cos = (sincos[:, i].unsqueeze(2).to_broadcast([P, TOK, heads, HALF]) for i in range(2))
                part = [rot[:, i, :, 0:heads, :] for i in range(4)]
                nc.vector.tensor_tensor(part[0], t1, cos, ALU.mult)
                nc.vector.tensor_tensor(part[1], t2, sin, ALU.mult)
                nc.vector.tensor_tensor(part[2], t2, cos, ALU.mult)
                link(nc.vector.tensor_tensor(part[3], t1, sin, ALU.mult))
                nc.vector.tensor_tensor(t1, part[0], part[1], ALU.subtract)
                nc.vector.tensor_tensor(t2, part[2], part[3], ALU.add).then_inc(rotated, 1)

            dve.wait_ge(sincos_made, 1)
            dve.wait_ge(qkv_evac, 2)
            rotate(k_sb.rearrange("p t (h d) -> p t h d", h=GROUP), GROUP)

            split_ahead(B_Q, 0)
            dve.wait_ge(acc_free, 2 * B_KV + 2)
            nc.vector.tensor_copy(v_band[0:CHUNK, 1, :], v_band[CHUNK:P, 0, :])
            link(nc.vector.tensor_copy(v_band[CHUNK:P, 1, :], v_band[0:CHUNK, 2, :]))
            for pair in range(1, PAIRS):
                split_ahead(B_Q, pair)

            def rotate_q(blk):
                dve.wait_ge(acc_free, blk * 2 + 2)
                rotate(s[:, :, :].rearrange("p t (h d) -> p t h d", h=GROUP), GROUP)

            rotate_q(B_Q)

            def copy_cur(g):
                nc.vector.tensor_copy(k_cur, kT[:, bass.ds(g, 1), :].rearrange("p g n -> p (g n)"))
                nc.vector.tensor_copy(v_cur, v_band[:, :, bass.ds(g * HD, HD)])

            def copy_qT(g):
                dve.wait_ge(qt_filled, g * 2 + 2)
                nc.vector.tensor_copy(qT[:, 2:4, :, :].rearrange("p c h n -> p h c n"),
                                      tb[1][:, :].rearrange("p (h c n) -> p h c n", h=PAIRED, c=2)
                                      ).then_inc(qt_copied_dve, 1)

            def row_max(g, half):
                sink = neg_sink[:, bass.ds(g, 1), :, :].rearrange("p g e a -> p g (e a)").to_broadcast([P, 2, PAIRED])
                dve.wait_ge(scores_made, g * 2 + (half + 1))
                for i in range(2):
                    nk, _ = keys(2 * half + i)
                    rows = scores[:, :, 2 * i * P:(2 * i + 2) * P].rearrange("p e (a n) -> p e a n", a=2)[:, :, :, 0:nk]
                    last = nc.vector.tensor_reduce(mx[:, i, :].rearrange("p (e a) -> p e a", e=2), rows, AX_X, ALU.max)
                link(last)
                link(nc.vector.scalar_tensor_tensor(out=neg_max[:, :, :], in0=mx[:, :, :], scalar=-SCALE,
                                                    in1=sink, op0=ALU.mult, op1=ALU.min))
                nc.vector.tensor_tensor(sink_arg[:, :, :], neg_max[:, :, :], sink, ALU.subtract
                                        ).then_inc(max_made, 1)

            def normalise(g, half):
                dve.wait_ge(exp_made, g * 2 + (half + 1))
                link(nc.vector.tensor_tensor(den[:, :, :], p_sum[:, :, :], sink_exp[:, :, :], ALU.add))
                link(nc.vector.reciprocal(r_den[:, :, :], den[:, :, :]))
                for i in range(2):
                    nk, _ = keys(2 * half + i)
                    p = probs[:, i, :].rearrange("p (m n) -> p m n", m=PAIRED)[:, :, 0:nk]
                    last = nc.vector.tensor_tensor(p, p, r_den[:, i, :].unsqueeze(2).to_broadcast([P, PAIRED, nk]),
                                                   ALU.mult)
                last.then_inc(probs_made, 1)

            def split_o(g, half):
                dve.wait_ge(o_hi, g * 2 + (half + 1))
                for i in range(2):
                    c = 2 * half + i
                    at = (slice(None), bass.ds(g * PAIRED, PAIRED), slice(c * CHUNK, (c + 1) * CHUNK))
                    last = nc.vector.tensor_tensor(b_lo[at], ob[i][:, 0:256].rearrange("p (h n) -> p h n", h=PAIRED),
                                                   b_hi[at].bitcast(F32), ALU.subtract)
                last.then_inc(o_lo, 1)

            LINKS = 2 * 4 + 1

            def attend(blk, g, evac):
                split_ahead(blk, 0)
                copy_cur(g)
                copy_qT(g)
                split_ahead(blk, 1)
                row_max(g, 0)
                normalise(g, 0)
                split_ahead(blk, 2)
                row_max(g, 1)
                split_o(g, 0)
                normalise(g, 1)
                if evac:
                    split_ahead(blk, 3)
                split_o(g, 1)
                if evac:
                    rotate_q(blk)
                else:
                    split_ahead(blk, 3)

            dve.wait_ge(kt_copied, 2)
            with chain.loop(0, KVH - 1, LINKS) as g:
                attend(g + (B_Q + 1), g, True)
            attend(B_WO, KVH - 1, False)
            to_y(B_WO, 0, False)
            dve.wait_ge(row_landed[0], 16)
            for t in range(TOK):
                scale_y(0, t, 0, 0)
            finish_y(B_WO, False, 0, 0)
            mlp(B_MLP0, 0, UNITS, 1, 2 * NB)

            first_block(B_V, T_V, 4)

            def v_stats(j):
                for t in range(TOK):
                    dve.wait_ge(acc_free, j * 2 + (2 * B_V + t + 1))
                    nc.vector.bn_stats(stats[:, t, bass.ds(j, 1), :].rearrange("p a n -> p (a n)"),
                                       y[:, t, bass.ds(j * COL, COL)]).then_inc(dve_chain, 1)
                    chain.n = chain.n + 1

            v_stats(0)
            with chain.loop(1, NB, TOK) as j:
                for pair in range(PAIRS):
                    split_ahead(j + B_V, pair)
                v_stats(j)
            dve.wait_ge(dve_chain, chain.n)
            for t in range(TOK):
                last = nc.vector.bn_aggr(moments[:, t, :], stats[:, t].rearrange("p j n -> p (j n)"))
            link(last)
            norms[0] += 1
            nc.vector.tensor_scalar(mean_sq[:, :], moments[:, :, 1], EPS, None, ALU.add).then_inc(norm_mean, 1)
            split_ahead(B_U, 0)
            inverse(r_out[:, :])
            dve.wait_ge(norm_done, norms[0])
            dve.wait_ge(row_landed[2], 16)
            dve.wait_ge(row_landed[3], 16)

            def layer_norm(c):
                f = slice(c * COL, (c + 1) * COL)
                for t in range(TOK):
                    last = nc.vector.tensor_scalar(y[:, t, f], y[:, t, f], moments[:, t, 0:1], r_out[:, t:t + 1],
                                                   ALU.subtract, ALU.mult)
                link(last)
                for t in range(TOK):
                    last = nc.vector.tensor_tensor(y[:, t, f], y[:, t, f], gain[:, 0, f], ALU.mult)
                link(last)
                for t in range(TOK):
                    nc.vector.tensor_tensor(y[:, t, f], y[:, t, f], lnb[:, f], ALU.add).then_inc(normed, 1)

            def gates_to_y(c):
                for t in range(TOK):
                    dve.wait_ge(gates_made, 2 * c + t + 1)
                    for i in range(2):
                        g = 2 * c + i
                        last = nc.vector.tensor_scalar(y[:, t, g * SGD:(g + 1) * SGD], sc[t][:, i * SGD:(i + 1) * SGD],
                                                       bs_cols[:, g:g + 1], None, ALU.add)
                    last.then_inc(gates_ready, 1)

            def apply_gates(j):
                for t in range(TOK):
                    dve.wait_ge(acc_free, j * 2 + (2 * B_U + t + 1))
                    nc.vector.tensor_tensor(s[:, t, :], s[:, t, :], y[:, t, bass.ds(j * COL, COL)], ALU.mult
                                            ).then_inc(gated, 1)

            layer_norm(0)
            for pair in range(1, PAIRS):
                split_ahead(B_U, pair)
                layer_norm(pair)
                gates_to_y(pair - 1)
            gates_to_y(3)
            dve.wait_ge(gates_ready, 2 * NB)
            apply_gates(0)
            with dve.Fori(1, NB) as j:
                split_ahead(j + B_U, 0)
                for t in range(TOK):
                    split_s(t, (j - 1) * 2 + (T_U + t), (j - 1) * 4)
                for pair in range(1, PAIRS):
                    split_ahead(j + B_U, pair)
                apply_gates(j)
            split_ahead(B_OUT, 0)
            for t in range(TOK):
                split_s(t, 2 * (NB - 1) + T_U + t, 4 * (NB - 1))
            for pair in range(1, PAIRS):
                split_ahead(B_OUT, pair)
            to_y(B_OUT, 0, False)
            dve.wait_ge(row_landed[4], 16)
            for t in range(TOK):
                scale_y(0, t, 1, 4 * NB)
            finish_y(B_OUT, False, 1, 4 * NB)
            mlp(B_MLP1, 1, T_MLP1 - UNITS, 0, 6 * NB)

            dve.wait_ge(norm_done, norms[0])
            for c in range(NB):
                f = slice(c * COL, (c + 1) * COL)
                for t in range(TOK):
                    last = nc.vector.scalar_tensor_tensor(out=h[:, t, f], in0=y[:, t, f], scalar=r_out[:, t:t + 1],
                                                          in1=h[:, t, f], op0=ALU.mult, op1=ALU.add)
                last.then_inc(out_ready, 1)


INS = ("x", "positions", "norm_gains", "attn_w_qkv", "attn_w_o", "attn_sinks", "sgu_w_in", "sgu_ln_g", "sgu_ln_b",
       "sgu_w_s", "sgu_b_s", "sgu_w_out", "mlp_w_up", "mlp_w_down")


def kernel(**inputs):
    import concourse.bacc as bacc
    from concourse.bass_utils import run_bass_kernel_spmd

    nc = bacc.Bacc("TRN2", target_bir_lowering=False, num_devices=1)
    arrays, args = {}, []
    for name in INS:
        a = np.ascontiguousarray(inputs[name])
        arrays[f"in_{name}"] = a
        args.append(nc.dram_tensor(f"in_{name}", a.shape, mybir.dt.from_np(a.dtype), kind="ExternalInput").ap())
    out = nc.dram_tensor("out_0", arrays["in_x"].shape, F32, kind="ExternalOutput").ap()
    trunk(nc, *args, out)
    r = run_bass_kernel_spmd(nc, [arrays], core_ids=[0])
    return r.results[0]["out_0"]
```

```python
import math
from contextlib import ExitStack, contextmanager

import numpy as np

import concourse.bass as bass
from concourse import mybir

F32 = mybir.dt.float32
F32R = mybir.dt.float32r
I32 = mybir.dt.int32
ALU = mybir.AluOpType
ACT = mybir.ActivationFunctionType
AX_X = mybir.AxisListType.X

P = 128
SEQ = 256
TOK = SEQ // P
D = 2048
KB = D // P
COL = 512
NB = D // COL
SLAB_KB = 2
SLAB = SLAB_KB * COL
RAW_SLOTS = 4
SLOTS = 8
LEAD = 3
PAIRS = KB // SLAB_KB // 2
QUARTERS = 4
HEADS, HD, KVH = 32, 64, 4
GROUP = HEADS // KVH
PAIRED = GROUP // 2
CHUNK = 64
ROT = HD // 4
HALF = ROT // 2
THETA = 500000.0
SG = 8
SGD = D // SG
EPS = 1e-6
SCALE = 1.0 / math.sqrt(HD)
UNIT = [(0, 0), (1, 0), (2, 0), (0, 1), (1, 1), (2, 1), (3, 0), (3, 1)]
UNITS = len(UNIT)

B_KV, B_Q, B_WO = 0, 1, 5
B_MLP0 = B_WO + NB
B_V = B_MLP0 + 2 * NB * QUARTERS
B_U, B_OUT = B_V + NB, B_V + 2 * NB
B_MLP1 = B_V + 3 * NB
BLOCKS = B_MLP1 + 2 * NB * QUARTERS

T_MLP0 = 2 * UNITS
T_V = T_MLP0 + 2 * NB * QUARTERS
T_U = T_V + UNITS
T_MLP1 = T_U + 2 * NB + UNITS

TWO_PI = 2 * math.pi
PI_1 = 6.28125
PI_2 = float(np.float32(math.floor((TWO_PI - PI_1) * 2.0 ** 19) / 2.0 ** 19))
PI_3 = float(np.float32(TWO_PI - PI_1 - PI_2))
ROUNDER = 1.5 * 2.0 ** 23
PI_MAX = float(np.nextafter(np.float32(math.pi), np.float32(0)))


class Chain:

    def __init__(self, eng, sem):
        self.eng, self.sem, self.n = eng, sem, 0

    def link(self, ins):
        self.n = self.n + 1
        ins.then_inc(self.sem, 1)
        self.eng.wait_ge(self.sem, self.n)

    @contextmanager
    def loop(self, start, end, links):
        before = self.n
        with self.eng.Fori(start, end) as i:
            self.n = (i - start) * links + before
            yield i
        self.n = before + (end - start) * links


def trunk(nc, x, positions, gains, w_qkv, w_o, sinks, w_in, ln_g, ln_b, w_s, b_s, w_out, w_up, w_down, out):
    ctx = ExitStack()
    with ctx:
        def sb(name, shape, dt=F32):
            return ctx.enter_context(nc.sbuf_tensor(name, shape, dt))

        def bank(name):
            return ctx.enter_context(nc.psum_tensor(name, [P, COL], F32))

        def sem(name):
            return ctx.enter_context(nc.semaphore(name))

        h = sb("h", [P, TOK, D])
        y = sb("y", [P, TOK, D])
        a_hi = sb("a_hi", [P, KB, SEQ], F32R)
        a_lo = sb("a_lo", [P, KB, SEQ], F32R)
        b_hi = sb("b_hi", [P, KB, SEQ], F32R)
        b_lo = sb("b_lo", [P, KB, SEQ], F32R)
        w_raw = sb("w_raw", [P, RAW_SLOTS, SLAB])
        w_hi = sb("w_hi", [P, SLOTS, SLAB], F32R)
        w_lo = sb("w_lo", [P, SLOTS, SLAB], F32R)
        gain = sb("gain", [P, D])
        s = sb("s", [P, TOK, COL])
        work = sb("work", [P, 3072])
        ident = sb("ident", [P, P])
        gain_rows = sb("gain_rows", [P, P])
        gain_cols = sb("gain_cols", [P, 8 * KB])
        warm = sb("warm", [P, 1])
        bs_rows = sb("bs_rows", [SG, P])
        bs_cols = sb("bs_cols", [P, SG])
        ssq = sb("ssq", [P, TOK, NB])
        pre_ssq = sb("pre_ssq", [P, 2, TOK])
        sum_sq = sb("sum_sq", [P, TOK])
        mean_sq = sb("mean_sq", [P, TOK])
        root = sb("root", [P, TOK])
        r_in = sb("r_in", [P, TOK])
        r_out = sb("r_out", [P, TOK])
        pos_i = sb("pos_i", [P, TOK], I32)
        pos_f = sb("pos_f", [P, TOK])
        freq = sb("freq", [P, HALF])
        ang = sb("ang", [P, TOK, HALF])
        turns = sb("turns", [P, 2, TOK, HALF])
        red = sb("red", [P, 2, TOK, HALF])
        sincos = sb("sincos", [P, 2, TOK, HALF])
        rot = sb("rot", [P, 4, TOK, GROUP, HALF])
        sink_rows = sb("sink_rows", [P, KVH * 2, 2])
        neg_sink = sb("neg_sink", [P, KVH, 2, 2])
        mx = sb("mx", [P, 2, PAIRED])
        neg_max = sb("neg_max", [P, 2, PAIRED])
        sink_arg = sb("sink_arg", [P, 2, PAIRED])
        sink_exp = sb("sink_exp", [P, 2, PAIRED])
        p_sum = sb("p_sum", [P, 2, PAIRED])
        den = sb("den", [P, 2, PAIRED])
        r_den = sb("r_den", [P, 2, PAIRED])
        stats = sb("stats", [P, TOK, NB, 6])
        moments = sb("moments", [P, TOK, 2])

        yf = y[:, :, :].rearrange("p t n -> p (t n)")
        k_sb = yf[:, 0:1024].rearrange("p (t n) -> p t n", t=TOK)
        kT = yf[:, 1024:2048].rearrange("p (g n) -> p g n", g=KVH)
        qT = yf[:, 2048:3072].rearrange("p (c h n) -> p c h n", c=4, h=PAIRED)
        k_cur = yf[:, 3072:3072 + SEQ]
        probs = [buf[:, 0:1024].rearrange("p (b n) -> p b n", b=2) for buf in (work, gain)]
        pT = work[:, 1024:2048].rearrange("p (b n) -> p b n", b=2)
        v_band = work[:, 2048:2816].rearrange("p (v n) -> p v n", v=3)
        v_cur = work[:, 2816:3008].rearrange("p (v n) -> p v n", v=3)
        ws_raw = s[:, :, :].rearrange("p t (g n) -> p (t g) n", n=P)
        lnb = work[:, 0:D]
        wsT = work[:, D:D + SG * P].rearrange("p (g n) -> p g n", g=SG)

        acc = [bank("acc0"), bank("acc1")]
        tb = [bank("t0"), bank("t1")]
        scores = ctx.enter_context(nc.psum_tensor("scores", [P, 2, COL], F32))
        sc = [scores[:, 0, :], scores[:, 1, :]]
        ob = [bank("o0"), bank("o1")]
        junk = ob[1]

        x_landed = [sem(f"x_landed{i}") for i in range(UNITS)]
        gains_landed = sem("gains_landed")
        pos_landed = sem("pos_landed")
        sinks_landed = sem("sinks_landed")
        ws_landed = sem("ws_landed")
        row_landed = [sem(f"row_landed{i}") for i in range(6)]
        slab_landed = [sem(f"slab_landed{i}") for i in range(RAW_SLOTS)]
        out_stored = sem("out_stored")
        consts_made = sem("consts_made")
        hi_made = sem("hi_made")
        lo_made = sem("lo_made")
        slab_used = sem("slab_used")
        half_done = sem("half_done")
        acc_free = sem("acc_free")
        t_filled = sem("t_filled")
        t_hi = sem("t_hi")
        t_lo = sem("t_lo")
        h_ready = sem("h_ready")
        squared = sem("squared")
        y_squared = sem("y_squared")
        y_scaled = sem("y_scaled")
        norm_sum = sem("norm_sum")
        norm_mean = sem("norm_mean")
        norm_root = sem("norm_root")
        norm_done = sem("norm_done")
        small_filled = sem("small_filled")
        small_copied = sem("small_copied")
        angles_made = sem("angles_made")
        sincos_made = sem("sincos_made")
        qkv_evac = sem("qkv_evac")
        rotated = sem("rotated")
        kt_filled = sem("kt_filled")
        kt_copied = sem("kt_copied")
        qt_filled = sem("qt_filled")
        qt_copied_act = sem("qt_copied_act")
        qt_copied_dve = sem("qt_copied_dve")
        cur_copied = sem("cur_copied")
        scores_made = sem("scores_made")
        max_made = sem("max_made")
        exp_made = sem("exp_made")
        probs_made = sem("probs_made")
        pt_filled = sem("pt_filled")
        pt_copied = sem("pt_copied")
        o_filled = sem("o_filled")
        o_hi = sem("o_hi")
        o_lo = sem("o_lo")
        ws_masked = sem("ws_masked")
        normed = sem("normed")
        gates_made = sem("gates_made")
        gates_ready = sem("gates_ready")
        gated = sem("gated")
        out_ready = sem("out_ready")
        dve_chain = sem("dve_chain")

        block = ctx.enter_context(nc.Block())

        def at_least(eng, sem_, value):
            if not isinstance(value, int) or value > 0:
                eng.wait_ge(sem_, value)

        def product_done(eng, blk, t):
            if t == 0:
                eng.wait_ge(half_done, blk + 1)
            else:
                eng.wait_ge(slab_used, (blk + 1) * (2 * PAIRS))

        def keys(c):
            return (CHUNK, 0) if c == 0 else (2 * CHUNK, (c - 1) * CHUNK)

        def slab_ahead(blk, i):
            i = i + 2 * LEAD
            return (blk, i) if i < 2 * PAIRS else (blk + 1, i - 2 * PAIRS)

        @block.sync
        def _(sp):
            def load_x(n):
                pair, t = UNIT[n]
                f = slice(pair * COL, (pair + 1) * COL)
                sp.dma_start(h[:, t, f], x[0].rearrange("(t p) n -> p t n", p=P)[:, t, f]).then_inc(x_landed[n], 16)

            def load_block(blk, w, col, kb0=0, slabs=range(2 * PAIRS)):
                rows = w.rearrange("(k p) n -> p k n", p=P)
                for i in slabs:
                    at_least(sp, lo_made, blk * (2 * PAIRS) + (i + 1 - RAW_SLOTS))
                    src = rows[:, bass.ds(kb0 + i * SLAB_KB, SLAB_KB), bass.ds(col, COL)]
                    sp.dma_start(w_raw[:, i % RAW_SLOTS, :].rearrange("p (k n) -> p k n", k=SLAB_KB), src
                                 ).then_inc(slab_landed[i % RAW_SLOTS], 16)

            def load_mlp(base, layer):
                for q0, q1 in ((0, 1), (1, QUARTERS)):
                    with sp.Fori(q0, q1) as q:
                        with sp.Fori(0, NB) as j:
                            load_block(q * (2 * NB) + j + base, w_up[layer], q * D + j * COL)
                        with sp.Fori(0, NB) as j:
                            load_block(q * (2 * NB) + j + (base + NB), w_down[layer], j * COL, q * KB)

            for units, slabs in (([0], (0, 2)), ([1], (2, 3)), ([2, 3], (3, 4)), ([4], (4, 6)), ([5, 6, 7], (6, 8))):
                for n in units:
                    load_x(n)
                load_block(B_KV, w_qkv[0], D, slabs=range(*slabs))
            with sp.Fori(0, NB) as j:
                load_block(j + B_Q, w_qkv[0], j * COL)
            with sp.Fori(0, NB) as j:
                load_block(j + B_WO, w_o[0], j * COL)
            load_mlp(B_MLP0, 0)
            with sp.Fori(0, NB) as j:
                load_block(j + B_V, w_in[0], j * COL + D)
            with sp.Fori(0, NB) as j:
                load_block(j + B_U, w_in[0], j * COL)
            with sp.Fori(0, NB) as j:
                load_block(j + B_OUT, w_out[0], j * COL)
            load_mlp(B_MLP1, 1)
            for n in range(UNITS):
                t, c = n // NB, n % NB
                f = slice(c * COL, (c + 1) * COL)
                sp.wait_ge(out_ready, n + 1)
                sp.dma_start(out[0, t * P:(t + 1) * P, f], h[:, t, f]).then_inc(out_stored, 16)
            sp.wait_ge(out_stored, 16 * UNITS)

        @block.gpsimd
        def _(pool):
            nc.gpsimd.memset(ident[:, :], 0.0).then_inc(consts_made, 1)
            pool.wait_ge(consts_made, 1)
            nc.gpsimd.affine_select(out=ident[:, :], in_=ident[:, :], compare_op=ALU.not_equal, fill=1.0,
                                    base=0, pattern=[[-1, P]], channel_multiplier=1).then_inc(consts_made, 1)
            for i in range(HALF):
                f = float(np.float32(THETA) ** np.float32(-2.0 * i / ROT))
                nc.gpsimd.memset(freq[:, i:i + 1], f).then_inc(consts_made, 1)

            def load_row(n, dst, row):
                pool.dma_start(dst, row.partition_broadcast(P)).then_inc(row_landed[n], 16)

            pool.wait_ge(pt_filled, 2 * KVH)
            load_row(0, gain[:, :], gains[0, 1])
            pool.dma_start(bs_rows[:, :], b_s[0]).then_inc(ws_landed, 16)
            pool.wait_ge(y_scaled, 2 * NB)
            load_row(1, gain[:, :], gains[0, 3])
            load_row(3, lnb, ln_b[0])
            nc.gpsimd.memset(wsT[CHUNK:P, :, 0:CHUNK], 0.0).then_inc(ws_masked, 1)
            pool.wait_ge(y_scaled, 4 * NB)
            pool.wait_ge(h_ready, 2 * UNITS)
            load_row(2, gain[:, :], ln_g[0])
            pool.dma_start(ws_raw, w_s[0].rearrange("g i j -> i g j")).then_inc(ws_landed, 16)
            pool.wait_ge(normed, 2 * NB)
            load_row(4, gain[:, :], gains[1, 1])
            pool.wait_ge(y_scaled, 6 * NB)
            load_row(5, gain[:, :], gains[1, 3])

        @block.tensor
        def _(pe):
            def multiply_slab(blk, x_hi, x_lo, i, t):
                if i == 0:
                    at_least(pe, acc_free, blk * 2 + (t - 1))
                if t == 0:
                    pe.wait_ge(lo_made, blk * (2 * PAIRS) + (i + 1))
                for k in range(SLAB_KB):
                    kb = i * SLAB_KB + k
                    tok = slice(t * P, (t + 1) * P)
                    col = slice(k * COL, (k + 1) * COL)
                    w1, w2 = w_hi[:, i % SLOTS, col], w_lo[:, i % SLOTS, col]
                    nc.tensor.matmul(acc[t][:, :], lhsT=x_hi[:, kb, tok], rhs=w1, start=(kb == 0), stop=False)
                    nc.tensor.matmul(acc[t][:, :], lhsT=x_hi[:, kb, tok], rhs=w2, start=False, stop=False)
                    last = nc.tensor.matmul(acc[t][:, :], lhsT=x_lo[:, kb, tok], rhs=w1,
                                            start=False, stop=(kb == KB - 1))
                if t == 1:
                    last.then_inc(slab_used, 1)
                elif i == 2 * PAIRS - 1:
                    last.then_inc(half_done, 1)

            def multiply(blk, x_hi, x_lo, pair, t, between=None):
                multiply_slab(blk, x_hi, x_lo, 2 * pair, t)
                if between:
                    between()
                multiply_slab(blk, x_hi, x_lo, 2 * pair + 1, t)

            def transpose_s(t, use, ready, count):
                pe.wait_ge(ready, count)
                at_least(pe, t_lo, (use - 1) * 4)
                for k in range(4):
                    last = nc.tensor.transpose(tb[t][:, k * P:(k + 1) * P], s[:, t, k * P:(k + 1) * P], ident[:, :])
                last.then_inc(t_filled, 1)

            def transpose_unit(n, use0, first_layer=False):
                pair, t = UNIT[n]
                if first_layer:
                    pe.wait_ge(x_landed[n], 16)
                else:
                    pe.wait_ge(h_ready, h_base[0] + n + 1)
                at_least(pe, t_lo, (use0 + n - 1) * 4)
                for k in range(4):
                    f = (4 * pair + k) * P
                    last = nc.tensor.transpose(tb[n % 2][:, k * P:(k + 1) * P], h[:, t, f:f + P], ident[:, :])
                last.then_inc(t_filled, 1)

            def last_block(blk, use0=None):
                for pair in (0, 1):
                    for t in range(TOK):
                        multiply(blk, b_hi, b_lo, pair, t)
                for t in range(TOK):
                    for i in range(4, 8):
                        if t == 1 and i == 7 and use0 is not None:
                            transpose_unit(0, use0)
                        multiply_slab(blk, b_hi, b_lo, i, t)
                if use0 is not None:
                    transpose_unit(1, use0)

            def first_block(blk, use0, first_layer=False):
                order = [(t, i) for t in range(TOK) for i in range(6)] + [(t, i) for t in range(TOK) for i in (6, 7)]
                units = {0: 2, 2: 3, 4: 4, 6: 5, 8: 6, 10: 7}
                if first_layer:
                    transpose_unit(0, use0, True)
                    transpose_unit(1, use0, True)
                for step, (t, i) in enumerate(order):
                    pe.wait_ge(t_lo, (use0 + UNIT.index((i // 2, t))) * 4 + (i % 2 + 1) * SLAB_KB)
                    multiply_slab(blk, a_hi, a_lo, i, t)
                    if step in units:
                        transpose_unit(units[step], use0, first_layer)
                h_base[0] += 0 if first_layer else UNITS

            h_base = [0]

            def plain_block(blk, x_hi, x_lo, hooks=None, between=None):
                for pair in range(PAIRS):
                    for half in range(TOK):
                        multiply(blk, x_hi, x_lo, pair, half, (between or {}).get((pair, half)))
                        for step in (hooks or {}).get((pair, half), ()):
                            step()

            def transpose_q(g, t):
                pe.wait_ge(rotated, g * TOK + (t + 2))
                for hp in range(PAIRED):
                    last = nc.tensor.transpose(tb[t][:, hp * P:(hp + 1) * P], s[:, t, hp * P:(hp + 1) * P],
                                               ident[:, :])
                last.then_inc(qt_filled, 1)

            def score(g, half):
                if half == 0:
                    pe.wait_ge(qt_copied_act, g + 1)
                    pe.wait_ge(cur_copied, g + 1)
                else:
                    pe.wait_ge(qt_copied_dve, g + 1)
                    pe.wait_ge(exp_made, g * 2 + 1)
                for i in range(2):
                    c = 2 * half + i
                    nk, k0 = keys(c)
                    for e in range(2):
                        for a in range(2):
                            row = slice(e * HD, (e + 1) * HD)
                            last = nc.tensor.matmul(scores[:, e, (2 * i + a) * P:(2 * i + a) * P + nk],
                                                    lhsT=qT[row, c, 2 * a:2 * a + 2, :].rearrange("p h n -> p (h n)"),
                                                    rhs=k_cur[row, k0:k0 + nk], start=True, stop=True)
                last.then_inc(scores_made, 1)

            def transpose_p(g, half):
                pe.wait_ge(probs_made, g * 2 + (half + 1))
                for i in (1, 0):
                    nk, _ = keys(2 * half + i)
                    for m in range(PAIRED):
                        last = nc.tensor.transpose(tb[i][0:nk, m * P:(m + 1) * P],
                                                   probs[half][:, i, m * P:m * P + nk], ident[:, :])
                last.then_inc(pt_filled, 1)

            def weigh_v(g, half):
                pe.wait_ge(pt_copied, g * 2 + (half + 1))
                at_least(pe, o_lo, g * 2 + half)
                for i in (1, 0):
                    c = 2 * half + i
                    nk, _ = keys(c)
                    for e in range(2):
                        last = nc.tensor.matmul(ob[i][e * HD:(e + 1) * HD, 0:256], lhsT=v_cur[0:nk, (0, 0, 1, 2)[c], :],
                                                rhs=pT[0:nk, i, e * 256:(e + 1) * 256], start=True, stop=True)
                last.then_inc(o_filled, 1)

            def attend(blk, g, x_hi, x_lo, in_o=False):
                transpose_q(g, 0)
                steps = {
                    (0, 0): [lambda: transpose_q(g, 1), lambda: score(g, 0)],
                    (1, 0): [lambda: score(g, 1)],
                    (1, 1): [lambda: transpose_p(g, 0)],
                    (2, 0): [lambda: weigh_v(g, 0)],
                    (2, 1): [lambda: transpose_p(g, 1)],
                    (3, 0): [lambda: weigh_v(g, 1)],
                }
                between = {}
                if in_o:
                    steps[2, 1] += [lambda: pe.wait_ge(o_lo, 2 * KVH - 1)]
                    between[3, 0] = lambda: weigh_v(g, 1)
                    steps[3, 0] = [lambda: pe.wait_ge(o_lo, 2 * KVH)]
                plain_block(blk, x_hi, x_lo, steps, between)

            def mlp(base, layer, use0, then):
                def up_to_b(q, j, t):
                    use = q * (2 * NB) + j * 2 + (use0 + UNITS + t)
                    transpose_s(t, use, squared, q * (2 * NB) + j * 2 + (2 * NB * QUARTERS * layer + t + 1))

                def both(q, j):
                    return {(0, 0): [lambda: up_to_b(q, j, 0)], (0, 1): [lambda: up_to_b(q, j, 1)]}

                def quarter(q, blk, first, then=None, last=False):
                    if first:
                        first_block(blk, use0)
                    else:
                        plain_block(blk, a_hi, a_lo)
                    with pe.Fori(1, NB) as j:
                        plain_block(blk + j, a_hi, a_lo, both(q, j - 1))
                    down(q, blk + NB, 0, both(q, NB - 1))
                    with pe.Fori(1, NB - 1 if last else NB) as j:
                        down(q, blk + (NB + j), j, None)
                    if last:
                        last_block(blk + 2 * NB - 1, then)

                def down(q, blk, j, hooks):
                    for pair in range(PAIRS):
                        if hooks and pair == PAIRS - 1:
                            pe.wait_ge(t_lo, q * (8 * NB) + 4 * (use0 + UNITS + 2 * NB))
                        for half in range(TOK):
                            multiply(blk, b_hi, b_lo, pair, half)
                            for step in (hooks or {}).get((pair, half), ()):
                                step()

                quarter(0, base, True)
                with pe.Fori(1, QUARTERS - 1) as q:
                    quarter(q, q * (2 * NB) + base, False)
                quarter(QUARTERS - 1, base + (QUARTERS - 1) * 2 * NB, False, then, True)

            pe.wait_ge(consts_made, 2)
            pe.wait_ge(gains_landed, 16)
            nc.tensor.transpose(sc[0][:, 0:P], gain_rows[:, :], ident[:, :]).then_inc(small_filled, 1)

            first_block(B_KV, 0, first_layer=True)

            def transpose_k(t):
                pe.wait_ge(rotated, 1)
                for g in range(KVH):
                    last = nc.tensor.transpose(tb[t][:, g * P:(g + 1) * P], k_sb[:, t, g * P:(g + 1) * P],
                                               ident[:, :])
                last.then_inc(kt_filled, 1)

            plain_block(B_Q, a_hi, a_lo, {(1, 0): [lambda: transpose_k(0)], (1, 1): [lambda: transpose_k(1)]})
            pe.wait_ge(kt_copied, 2)
            with pe.Fori(0, KVH - 1) as g:
                attend(g + (B_Q + 1), g, a_hi, a_lo)
            pe.wait_ge(o_lo, 2 * (KVH - 1))
            attend(B_WO, KVH - 1, b_hi, b_lo, in_o=True)
            with pe.Fori(1, NB - 1) as j:
                plain_block(j + B_WO, b_hi, b_lo)
            last_block(B_WO + NB - 1, UNITS)
            mlp(B_MLP0, 0, UNITS, T_V)

            first_block(B_V, T_V)
            with pe.Fori(1, NB) as j:
                plain_block(j + B_V, a_hi, a_lo)

            def transpose_ws():
                pe.wait_ge(ws_landed, 32)
                for g in range(SG):
                    last = nc.tensor.transpose(sc[g // 4][:, (g % 4) * P:(g % 4 + 1) * P], ws_raw[:, g, :],
                                               ident[:, :])
                last.then_inc(small_filled, 1)
                nc.tensor.transpose(ob[0][:, 0:SG], bs_rows[:, :], ident[0:SG, 0:SG]).then_inc(small_filled, 1)

            def gate(c):
                for t in range(TOK):
                    pe.wait_ge(normed, 2 * c + t + 1)
                    at_least(pe, gates_ready, 2 * (c - 1) + t + 1)
                    for i in range(2):
                        g = 2 * c + i
                        last = nc.tensor.matmul(sc[t][:, i * SGD:(i + 1) * SGD], lhsT=wsT[:, g, :],
                                                rhs=y[:, t, g * SGD:(g + 1) * SGD], start=True, stop=True)
                    last.then_inc(gates_made, 1)

            def first_gates():
                pe.wait_ge(small_copied, 4)
                pe.wait_ge(ws_masked, 1)
                gate(0)

            plain_block(B_U, a_hi, a_lo, {
                (0, 0): [transpose_ws], (1, 0): [first_gates], (2, 0): [lambda: gate(1)],
                (3, 0): [lambda: gate(2)], (3, 1): [lambda: gate(3)]})

            def u_to_b(j, t):
                transpose_s(t, j * 2 + (T_U + t), gated, j * 2 + (t + 1))

            with pe.Fori(1, NB) as j:
                plain_block(j + B_U, a_hi, a_lo, {(0, 0): [lambda: u_to_b(j - 1, 0)],
                                                  (0, 1): [lambda: u_to_b(j - 1, 1)]})
            def gated_ready():
                pe.wait_ge(t_lo, 4 * (T_U + 2 * NB))
            plain_block(B_OUT, b_hi, b_lo, {(0, 0): [lambda: u_to_b(NB - 1, 0)],
                                            (0, 1): [lambda: u_to_b(NB - 1, 1)],
                                            (2, 1): [gated_ready]})
            with pe.Fori(1, NB - 1) as j:
                plain_block(j + B_OUT, b_hi, b_lo)
            last_block(B_OUT + NB - 1, T_MLP1 - UNITS)
            mlp(B_MLP1, 1, T_MLP1 - UNITS, None)

        @block.scalar
        def _(act):
            def split_slab(blk, i):
                act.wait_ge(slab_landed[i % RAW_SLOTS],
                            blk * (32 * PAIRS // RAW_SLOTS) + 16 * (i // RAW_SLOTS + 1))
                at_least(act, slab_used, blk * (2 * PAIRS) + (i + 1 - SLOTS))
                nc.scalar.activation(w_hi[:, i % SLOTS, :], w_raw[:, i % RAW_SLOTS, :], ACT.Copy).then_inc(hi_made, 1)

            def split_slabs(blk, pair):
                for i in (2 * pair, 2 * pair + 1):
                    split_slab(blk, i)

            def split_next(blk, *slabs):
                for i in slabs:
                    if not (isinstance(blk, int) and blk == BLOCKS - 1 and i + 2 * LEAD >= 2 * PAIRS):
                        split_slab(*slab_ahead(blk, i))

            def split_ahead(blk, pair):
                split_next(blk, 2 * pair, 2 * pair + 1)

            def split_unit(n, use0, norm):
                pair, t = UNIT[n]
                act.wait_ge(t_filled, use0 + n + 1)
                for k in range(4):
                    kb = 4 * pair + k
                    last = nc.scalar.activation(a_hi[:, kb, t * P:(t + 1) * P], tb[n % 2][:, k * P:(k + 1) * P],
                                                ACT.Copy, scale=gain_cols[:, norm * KB + kb:norm * KB + kb + 1])
                last.then_inc(t_hi, 1)

            def split_s(t, use, kb0):
                act.wait_ge(t_filled, use + 1)
                nc.scalar.activation(b_hi[:, bass.ds(kb0, 4), t * P:(t + 1) * P],
                                     tb[t][:, :].rearrange("p (k n) -> p k n", k=4), ACT.Copy).then_inc(t_hi, 1)

            def take_root(tok=slice(0, TOK)):
                norms[0] += 1
                act.wait_ge(norm_mean, norms[0])
                nc.scalar.activation(root[:, tok], mean_sq[:, tok], ACT.Sqrt).then_inc(norm_root, 1)

            norms = [0]

            def square_h(t, part):
                f = slice(part * D // 2, (part + 1) * D // 2)
                nc.scalar.activation(b_hi[:, 8 * part + 4 * t:8 * part + 4 * t + 4, :].rearrange("p k n -> p (k n)"),
                                     h[:, t, f], ACT.Square, accum_out=pre_ssq[:, part, t:t + 1]).then_inc(norm_sum, 1)

            def first_block(blk, use0, norm, evac, layer0=False):
                h0 = h_seen[0]
                h_seen[0] += 0 if layer0 else UNITS

                def square(t, part):
                    if layer0:
                        for pair in (2 * part, 2 * part + 1):
                            act.wait_ge(x_landed[UNIT.index((pair, t))], 16)
                    else:
                        act.wait_ge(h_ready, h0 + UNIT.index((2 * part + 1, t)) + 1)
                    square_h(t, part)

                if layer0:
                    split_unit(0, use0, norm)
                    split_slabs(0, 0)
                    split_unit(1, use0, norm)
                    split_slabs(0, 1)
                split_unit(2, use0, norm)
                if layer0:
                    split_slabs(0, 2)
                else:
                    split_ahead(blk - 1, 3)
                split_unit(3, use0, norm)
                if layer0:
                    split_ahead(blk, 0)
                split_unit(4, use0, norm)
                if not layer0:
                    split_next(blk, 0)
                square(0, 0)
                split_unit(5, use0, norm)
                split_next(blk, 2 if layer0 else 1)
                square(1, 0)
                split_unit(6, use0, norm)
                split_next(blk, 3 if layer0 else 2)
                square(0, 1)
                split_unit(7, use0, norm)
                square(1, 1)
                if not layer0:
                    split_next(blk, 3)
                take_root()
                act.wait_ge(norm_done, norms[0])
                evac(0)
                split_ahead(blk, 2)
                evac(1)
                split_ahead(blk, 3)

            h_seen = [0]

            def read_out(blk, t, dst, func):
                product_done(act, blk, t)
                return nc.scalar.activation(dst, acc[t][:, :], func, scale=r_in[:, t:t + 1])

            def square_y(blk, j, t, n):
                act.wait_ge(acc_free, blk * 2 + (t + 1))
                at_least(act, y_squared, j * TOK + (n + t))
                nc.scalar.activation(junk[:, :], y[:, t, bass.ds(j * COL, COL)], ACT.Square,
                                     accum_out=ssq[:, t, bass.ds(j, 1)]).then_inc(y_squared, 1)

            def product_to_y(base, j, n=None):
                for pair in range(PAIRS):
                    split_ahead(base + j, pair)
                if n is not None:
                    for t in range(TOK):
                        square_y(base + j, j, t, n)

            def last_block(blk, n, then=None):
                for pair in range(PAIRS - 1):
                    split_ahead(blk, pair)
                square_y(blk, NB - 1, 0, n)
                take_root(slice(0, 1))
                if then:
                    split_unit(0, *then)
                    split_unit(1, *then)
                square_y(blk, NB - 1, 1, n)
                take_root(slice(1, 2))

            def mlp(base, layer, use0, n, then):
                def up_tile(blk, t):
                    read_out(blk, t, s[:, t, :], ACT.Relu).then_inc(acc_free, 1)
                    act.wait_ge(acc_free, blk * 2 + (t + 1))
                    nc.scalar.activation(s[:, t, :], s[:, t, :], ACT.Square).then_inc(squared, 1)

                def up_evac(blk):
                    for t in range(TOK):
                        up_tile(blk, t)

                def up_splits(q, j):
                    for t in range(TOK):
                        split_s(t, q * (2 * NB) + j * 2 + (use0 + UNITS + t), j * 4)

                def quarter(q, blk, first, last):
                    if first:
                        first_block(blk, use0, 4 * layer + 2, lambda t: up_tile(blk, t))
                    else:
                        for pair in range(PAIRS):
                            split_ahead(blk, pair)
                        up_evac(blk)
                    with act.Fori(1, NB) as j:
                        split_ahead(blk + j, 0)
                        up_splits(q, j - 1)
                        for pair in range(1, PAIRS):
                            split_ahead(blk + j, pair)
                        up_evac(blk + j)
                    split_ahead(blk + NB, 0)
                    up_splits(q, NB - 1)
                    for pair in range(1, PAIRS):
                        split_ahead(blk + NB, pair)
                    if last:
                        for t in range(TOK):
                            square_y(blk + NB, 0, t, n)
                    if last:
                        with act.Fori(1, NB - 1) as j:
                            product_to_y(blk + NB, j, n)
                        last_block(blk + 2 * NB - 1, n, then)
                    else:
                        with act.Fori(1, NB) as j:
                            product_to_y(blk + NB, j)

                quarter(0, base, True, False)
                with act.Fori(1, QUARTERS - 1) as q:
                    quarter(q, q * (2 * NB) + base, False, False)
                quarter(QUARTERS - 1, base + (QUARTERS - 1) * 2 * NB, False, True)

            act.dma_start(gain_rows[:, :], gains.rearrange("l i (k p) -> (l i k) p", p=P)).then_inc(gains_landed, 16)
            act.wait_ge(consts_made, 2)
            nc.scalar.activation(warm[:, :], ident[:, 0:1], ACT.Sqrt)
            act.dma_start(pos_i[:, :], positions[0].rearrange("(t p) -> p t", p=P),
                          allow_slow_non_contiguous=True).then_inc(pos_landed, 16)
            for i in range(2):
                act.dma_start(sink_rows[i * CHUNK:(i + 1) * CHUNK, :, :],
                              sinks[0].rearrange("(a i e) -> i a e", i=2, e=2)[i].partition_broadcast(CHUNK),
                              allow_slow_non_contiguous=True).then_inc(sinks_landed, 16)
            act.wait_ge(small_filled, 1)
            nc.scalar.activation(gain_cols[:, :], sc[0][:, 0:P], ACT.Copy).then_inc(small_copied, 1)
            act.wait_ge(small_copied, 1)

            def kv_evac(t):
                product_done(act, B_KV, t)
                once = acc[t][:, 0:256].rearrange("p (g d) -> p g d", g=KVH)
                nc.scalar.activation(k_sb[:, t, :].rearrange("p (g e d) -> p g e d", g=KVH, e=2),
                                     once.unsqueeze(2).to_broadcast([P, KVH, 2, HD]), ACT.Copy,
                                     scale=r_in[:, t:t + 1]).then_inc(qkv_evac, 1)
                nc.scalar.activation(v_band[:, 2 * t, :], acc[t][:, 256:512], ACT.Copy, scale=r_in[:, t:t + 1]
                                     ).then_inc(acc_free, 1)

            first_block(B_KV, 0, 0, kv_evac, layer0=True)

            act.wait_ge(angles_made, 1)
            nc.scalar.activation(sincos[:, :, :, :], red[:, :, :, :], ACT.Sin).then_inc(sincos_made, 1)

            def q_evac(blk, t):
                read_out(blk, t, s[:, t, :], ACT.Copy).then_inc(acc_free, 1)

            split_ahead(B_Q, 0)
            split_ahead(B_Q, 1)
            for t in range(TOK):
                act.wait_ge(kt_filled, t + 1)
                nc.scalar.activation(kT[:, :, t * P:(t + 1) * P],
                                     tb[t][:, :].rearrange("p (g n) -> p g n", g=KVH), ACT.Copy
                                     ).then_inc(kt_copied, 1)
            for pair in range(2, PAIRS):
                split_ahead(B_Q, pair)
            for t in range(TOK):
                q_evac(B_Q, t)

            def copy_qT(g):
                act.wait_ge(qt_filled, g * 2 + 1)
                nc.scalar.activation(qT[:, 0:2, :, :].rearrange("p c h n -> p h c n"),
                                     tb[0][:, :].rearrange("p (h c n) -> p h c n", h=PAIRED, c=2), ACT.Copy
                                     ).then_inc(qt_copied_act, 1)

            def exponentials(g, half):
                act.wait_ge(max_made, g * 2 + (half + 1))
                for i in range(2):
                    nk, _ = keys(2 * half + i)
                    for m in range(PAIRED):
                        e, a = m // 2, m % 2
                        nc.scalar.activation(probs[half][:, i, m * P:m * P + nk],
                                             scores[:, e, (2 * i + a) * P:(2 * i + a) * P + nk], ACT.Exp,
                                             bias=neg_max[:, i, m:m + 1], scale=SCALE,
                                             accum_out=p_sum[:, i, m:m + 1])
                nc.scalar.activation(sink_exp[:, :, :], sink_arg[:, :, :], ACT.Exp).then_inc(exp_made, 1)

            def copy_pT(g, half):
                act.wait_ge(pt_filled, g * 2 + (half + 1))
                for i in range(2):
                    nk, _ = keys(2 * half + i)
                    last = nc.scalar.activation(pT[0:nk, i, :], tb[i][0:nk, :], ACT.Copy)
                last.then_inc(pt_copied, 1)

            def split_o(g, half):
                act.wait_ge(o_filled, g * 2 + (half + 1))
                for i in range(2):
                    c = 2 * half + i
                    last = nc.scalar.activation(b_hi[:, bass.ds(g * PAIRED, PAIRED), c * CHUNK:(c + 1) * CHUNK],
                                                ob[i][:, 0:256].rearrange("p (h n) -> p h n", h=PAIRED), ACT.Copy)
                last.then_inc(o_hi, 1)

            def attend(blk, g, evac):
                copy_qT(g)
                split_next(blk, 0, 1)
                exponentials(g, 0)
                split_next(blk, 2, 3)
                exponentials(g, 1)
                copy_pT(g, 0)
                split_next(blk, 4)
                split_o(g, 0)
                split_next(blk, 5, 6, 7)
                copy_pT(g, 1)
                if evac:
                    q_evac(blk, 0)
                split_o(g, 1)
                if evac:
                    q_evac(blk, 1)

            with act.Fori(0, KVH - 1) as g:
                attend(g + (B_Q + 1), g, True)
            attend(B_WO, KVH - 1, False)
            for t in range(TOK):
                square_y(B_WO, 0, t, 0)
            nc.scalar.activation(warm[:, :], ident[:, 0:1], ACT.Sqrt)
            with act.Fori(1, NB - 1) as j:
                product_to_y(B_WO, j, 0)
            last_block(B_WO + NB - 1, 0, (UNITS, 2))
            mlp(B_MLP0, 0, UNITS, 2 * NB, (T_V, 4))

            def v_tile(j, t):
                read_out(j + B_V, t, y[:, t, bass.ds(j * COL, COL)], ACT.Gelu_apprx_tanh).then_inc(acc_free, 1)

            def v_evac(j):
                for t in range(TOK):
                    v_tile(j, t)

            first_block(B_V, T_V, 4, lambda t: v_tile(0, t))
            with act.Fori(1, NB) as j:
                for pair in range(PAIRS):
                    split_ahead(j + B_V, pair)
                v_evac(j)

            def u_evac(j):
                for t in range(TOK):
                    read_out(j + B_U, t, s[:, t, :], ACT.Gelu_apprx_tanh).then_inc(acc_free, 1)

            split_ahead(B_U, 0)
            take_root()
            act.wait_ge(small_filled, 2)
            for i in range(2):
                full = sc[i][:, :].rearrange("p (g n) -> p g n", g=4)
                nc.scalar.activation(wsT[0:CHUNK, 4 * i:4 * i + 4, :], full[0:CHUNK], ACT.Copy)
                nc.scalar.activation(wsT[CHUNK:P, 4 * i:4 * i + 4, CHUNK:P], full[CHUNK:P, :, CHUNK:P],
                                     ACT.Copy).then_inc(small_copied, 1)
            act.wait_ge(small_filled, 3)
            nc.scalar.activation(bs_cols[:, :], ob[0][:, 0:SG], ACT.Copy).then_inc(small_copied, 1)
            for pair in range(1, PAIRS):
                split_ahead(B_U, pair)
            u_evac(0)
            with act.Fori(1, NB) as j:
                split_ahead(j + B_U, 0)
                for t in range(TOK):
                    split_s(t, (j - 1) * 2 + (T_U + t), (j - 1) * 4)
                for pair in range(1, PAIRS):
                    split_ahead(j + B_U, pair)
                u_evac(j)
            split_ahead(B_OUT, 0)
            for t in range(TOK):
                split_s(t, 2 * (NB - 1) + T_U + t, 4 * (NB - 1))
            for pair in range(1, PAIRS):
                split_ahead(B_OUT, pair)
            for t in range(TOK):
                square_y(B_OUT, 0, t, 4 * NB)
            nc.scalar.activation(warm[:, :], ident[:, 0:1], ACT.Sqrt)
            with act.Fori(1, NB - 1) as j:
                product_to_y(B_OUT, j, 4 * NB)
            last_block(B_OUT + NB - 1, 4 * NB, (T_MLP1 - UNITS, 6))
            mlp(B_MLP1, 1, T_MLP1 - UNITS, 6 * NB, None)

        @block.vector
        def _(dve):
            chain = Chain(dve, dve_chain)
            link = chain.link
            norms, sums, squares, seen_h = [0], [0], [0], [0]

            def split_slab(blk, i):
                dve.wait_ge(hi_made, blk * (2 * PAIRS) + (i + 1))
                nc.vector.tensor_tensor(w_lo[:, i % SLOTS, :], w_raw[:, i % RAW_SLOTS, :],
                                        w_hi[:, i % SLOTS, :].bitcast(F32), ALU.subtract).then_inc(lo_made, 1)

            def split_slabs(blk, pair):
                for i in (2 * pair, 2 * pair + 1):
                    split_slab(blk, i)

            def split_next(blk, *slabs):
                for i in slabs:
                    if not (isinstance(blk, int) and blk == BLOCKS - 1 and i + 2 * LEAD >= 2 * PAIRS):
                        split_slab(*slab_ahead(blk, i))

            def split_ahead(blk, pair):
                split_next(blk, 2 * pair, 2 * pair + 1)

            def split_unit(n, use0, norm):
                pair, t = UNIT[n]
                dve.wait_ge(t_hi, use0 + n + 1)
                for k in range(4):
                    kb = 4 * pair + k
                    tok = slice(t * P, (t + 1) * P)
                    nc.vector.scalar_tensor_tensor(
                        out=a_lo[:, kb, tok], in0=tb[n % 2][:, k * P:(k + 1) * P],
                        scalar=gain_cols[:, norm * KB + kb:norm * KB + kb + 1],
                        in1=a_hi[:, kb, tok].bitcast(F32), op0=ALU.mult, op1=ALU.subtract).then_inc(t_lo, 1)

            def split_s(t, use, kb0):
                dve.wait_ge(t_hi, use + 1)
                at = (slice(None), bass.ds(kb0, 4), slice(t * P, (t + 1) * P))
                nc.vector.tensor_tensor(b_lo[at], tb[t][:, :].rearrange("p (k n) -> p k n", k=4),
                                        b_hi[at].bitcast(F32), ALU.subtract).then_inc(t_lo, 4)

            def update_h(n, done=h_ready):
                pair, t = UNIT[n]
                f = slice(pair * COL, (pair + 1) * COL)
                last = pair == NB - 1
                nc.vector.scalar_tensor_tensor(out=h[:, t, f], in0=s[:, t, :] if last else y[:, t, f],
                                               scalar=r_out[:, t:t + 1],
                                               in1=h[:, t, f], op0=ALU.mult, op1=ALU.add).then_inc(done, 1)

            def mean(tok=slice(0, TOK)):
                norms[0] += 1
                nc.vector.tensor_scalar(mean_sq[:, tok], sum_sq[:, tok], 1.0 / D, EPS, ALU.mult, ALU.add
                                        ).then_inc(norm_mean, 1)

            def inverse(dst, tok=slice(0, TOK)):
                dve.wait_ge(norm_root, norms[0])
                nc.vector.reciprocal(dst[:, tok], root[:, tok]).then_inc(norm_done, 1)

            def first_block(blk, use0, norm, layer0=False):
                def update(n):
                    if not layer0:
                        update_h(n)

                if layer0:
                    split_unit(0, use0, norm)
                    split_slabs(0, 0)
                    split_unit(1, use0, norm)
                    split_slabs(0, 1)
                split_unit(2, use0, norm)
                if layer0:
                    split_slabs(0, 2)
                else:
                    split_ahead(blk - 1, 3)
                update(4)
                split_unit(3, use0, norm)
                if layer0:
                    split_ahead(blk, 0)
                update(5)
                split_unit(4, use0, norm)
                update(6)
                if not layer0:
                    split_next(blk, 0)
                split_unit(5, use0, norm)
                split_next(blk, 2 if layer0 else 1)
                update(7)
                split_unit(6, use0, norm)
                split_next(blk, 3 if layer0 else 2)
                split_unit(7, use0, norm)
                if not layer0:
                    split_next(blk, 3)
                sums[0] += 2 * TOK
                dve.wait_ge(norm_sum, sums[0])
                link(nc.vector.tensor_tensor(sum_sq[:, :], pre_ssq[:, 0, :], pre_ssq[:, 1, :], ALU.add))
                mean()
                inverse(r_in)
                if layer0:
                    rotary_angles()
                split_ahead(blk, 2)
                split_ahead(blk, 3)

            def tile_to_y(blk, j, add, t):
                dst = y[:, t, bass.ds(j * COL, COL)]
                product_done(dve, blk, t)
                if add:
                    nc.vector.tensor_tensor(dst, acc[t][:, :], dst, ALU.add).then_inc(acc_free, 1)
                else:
                    nc.vector.tensor_copy(dst, acc[t][:, :]).then_inc(acc_free, 1)

            def to_y(blk, j, add):
                for t in range(TOK):
                    tile_to_y(blk, j, add, t)

            def scale_y(j, t, n):
                dst = y[:, t, bass.ds(j * COL, COL)]
                dve.wait_ge(y_squared, j * TOK + (n + t + 1))
                nc.vector.tensor_tensor(dst, dst, gain[:, bass.ds(j * COL, COL)], ALU.mult).then_inc(y_scaled, 1)

            def scale_to_s(blk, t):
                dve.wait_ge(acc_free, 2 * blk + t + 1)
                nc.vector.tensor_tensor(s[:, t, :], y[:, t, D - COL:D], gain[:, D - COL:D], ALU.mult
                                        ).then_inc(y_scaled, 1)

            def product_to_y(blk0, j, add, n=None):
                for pair in range(PAIRS):
                    split_ahead(blk0 + j, pair)
                to_y(blk0 + j, j, add)
                if n is not None:
                    for t in range(TOK):
                        scale_y(j, t, n)

            def finish_y(blk0, add, n, then=None):
                with dve.Fori(1, NB - 1) as j:
                    product_to_y(blk0, j, add, n)
                blk = blk0 + NB - 1
                for pair in range(PAIRS - 1):
                    split_ahead(blk, pair)
                for t in range(TOK):
                    tok = slice(t, t + 1)
                    if t == 1 and then:
                        split_unit(0, *then)
                    tile_to_y(blk, NB - 1, add, t)
                    if not (t == 1 and then):
                        scale_to_s(blk, t)
                    else:
                        split_unit(1, *then)
                    dve.wait_ge(y_squared, n + 2 * (NB - 1) + t + 1)
                    link(nc.vector.tensor_reduce(sum_sq[:, tok], ssq[:, t, :], AX_X, ALU.add))
                    mean(tok)
                    if t == 1 and then:
                        scale_to_s(blk, t)
                    inverse(r_out, tok)
                    dve.wait_ge(norm_done, norms[0])
                    dve.wait_ge(y_scaled, n + 2 * (NB - 1) + t + 1)
                    for unit in range(3 * t, 3 * t + (3 if t == 0 or not then else 1)):
                        update_h(unit, h_ready if then else out_ready)
                    if not then:
                        update_h(UNIT.index((NB - 1, t)), out_ready)

            def mlp(base, layer, use0, n, then):
                def up_splits(q, j):
                    for t in range(TOK):
                        split_s(t, q * (2 * NB) + j * 2 + (use0 + UNITS + t), j * 4)

                def quarter(q, blk, first, last):
                    if first:
                        first_block(blk, use0, 4 * layer + 2)
                    else:
                        for pair in range(PAIRS):
                            split_ahead(blk, pair)
                    with dve.Fori(1, NB) as j:
                        split_ahead(blk + j, 0)
                        up_splits(q, j - 1)
                        for pair in range(1, PAIRS):
                            split_ahead(blk + j, pair)
                    split_ahead(blk + NB, 0)
                    up_splits(q, NB - 1)
                    for pair in range(1, PAIRS):
                        split_ahead(blk + NB, pair)
                    to_y(blk + NB, 0, not first)
                    if last:
                        for t in range(TOK):
                            scale_y(0, t, n)
                        finish_y(blk + NB, True, n, then)
                    else:
                        with dve.Fori(1, NB) as j:
                            product_to_y(blk + NB, j, not first)

                quarter(0, base, True, False)
                with dve.Fori(1, QUARTERS - 1) as q:
                    quarter(q, q * (2 * NB) + base, False, False)
                dve.wait_ge(row_landed[1 if layer == 0 else 5], 16)
                quarter(QUARTERS - 1, base + (QUARTERS - 1) * 2 * NB, False, True)

            def rotary_angles():
                dve.wait_ge(pos_landed, 16)
                dve.wait_ge(consts_made, 2 + HALF)
                link(nc.vector.tensor_copy(pos_f[:, :], pos_i[:, :]))
                for t in range(TOK):
                    last = nc.vector.tensor_scalar(ang[:, t, :], freq[:, :], pos_f[:, t:t + 1], None, ALU.mult)
                link(last)
                for i in range(2):
                    last = nc.vector.tensor_scalar(turns[:, i], ang[:, :, :], 1.0 / TWO_PI, 0.25 * i, ALU.mult, ALU.add)
                link(last)
                link(nc.vector.tensor_scalar(turns[:, :, :, :], turns[:, :, :, :], ROUNDER, None, ALU.add))
                link(nc.vector.tensor_scalar(turns[:, :, :, :], turns[:, :, :, :], ROUNDER, None, ALU.subtract))
                for n, part in enumerate((PI_1, PI_2, PI_3)):
                    for i in range(2):
                        last = nc.vector.scalar_tensor_tensor(
                            out=red[:, i], in0=turns[:, i], scalar=-part, in1=ang[:, :, :] if n == 0 else red[:, i],
                            op0=ALU.mult, op1=ALU.add)
                    link(last)
                link(nc.vector.tensor_scalar(red[:, 1], red[:, 1], math.pi / 2, None, ALU.add))
                nc.vector.tensor_scalar(red[:, :, :, :], red[:, :, :, :], PI_MAX, -PI_MAX, ALU.min, ALU.max
                                        ).then_inc(angles_made, 1)
                dve.wait_ge(sinks_landed, 32)
                link(nc.vector.tensor_scalar(neg_sink[:, :, :, :],
                                             sink_rows[:, :, :].rearrange("p (g a) e -> p g e a", a=2),
                                             -1.0, None, ALU.mult))

            dve.wait_ge(small_copied, 1)
            first_block(B_KV, 0, 0, layer0=True)

            def rotate(x, tiles, heads):
                t1, t2 = x[:, :, :, 0:HALF], x[:, :, :, HALF:ROT]
                n = tiles.stop - tiles.start
                sin, cos = (sincos[:, i, tiles].unsqueeze(2).to_broadcast([P, n, heads, HALF]) for i in range(2))
                part = [rot[:, i, tiles, 0:heads, :] for i in range(4)]
                nc.vector.tensor_tensor(part[0], t1, cos, ALU.mult)
                nc.vector.tensor_tensor(part[1], t2, sin, ALU.mult)
                nc.vector.tensor_tensor(part[2], t2, cos, ALU.mult)
                link(nc.vector.tensor_tensor(part[3], t1, sin, ALU.mult))
                nc.vector.tensor_tensor(t1, part[0], part[1], ALU.subtract)
                nc.vector.tensor_tensor(t2, part[2], part[3], ALU.add).then_inc(rotated, 1)

            dve.wait_ge(sincos_made, 1)
            dve.wait_ge(qkv_evac, 2)
            rotate(k_sb.rearrange("p t (h d) -> p t h d", h=GROUP), slice(0, TOK), GROUP)
            split_ahead(B_Q, 0)
            dve.wait_ge(acc_free, 2 * B_KV + 2)
            nc.vector.tensor_copy(v_band[0:CHUNK, 1, :], v_band[CHUNK:P, 0, :])
            link(nc.vector.tensor_copy(v_band[CHUNK:P, 1, :], v_band[0:CHUNK, 2, :]))
            for pair in range(1, PAIRS):
                split_ahead(B_Q, pair)

            def rotate_q(blk, t):
                dve.wait_ge(acc_free, blk * 2 + (t + 1))
                rotate(s[:, t:t + 1, :].rearrange("p t (h d) -> p t h d", h=GROUP), slice(t, t + 1), GROUP)

            rotate_q(B_Q, 0)
            rotate_q(B_Q, 1)

            def copy_cur(g):
                nc.vector.tensor_copy(k_cur, kT[:, bass.ds(g, 1), :].rearrange("p g n -> p (g n)"))
                nc.vector.tensor_copy(v_cur, v_band[:, :, bass.ds(g * HD, HD)]).then_inc(cur_copied, 1)

            def copy_qT(g):
                dve.wait_ge(qt_filled, g * 2 + 2)
                nc.vector.tensor_copy(qT[:, 2:4, :, :].rearrange("p c h n -> p h c n"),
                                      tb[1][:, :].rearrange("p (h c n) -> p h c n", h=PAIRED, c=2)
                                      ).then_inc(qt_copied_dve, 1)

            def row_max(g, half):
                sink = neg_sink[:, bass.ds(g, 1), :, :].rearrange("p g e a -> p g (e a)").to_broadcast([P, 2, PAIRED])
                dve.wait_ge(scores_made, g * 2 + (half + 1))
                for i in range(2):
                    nk, _ = keys(2 * half + i)
                    rows = scores[:, :, 2 * i * P:(2 * i + 2) * P].rearrange("p e (a n) -> p e a n", a=2)[:, :, :, 0:nk]
                    last = nc.vector.tensor_reduce(mx[:, i, :].rearrange("p (e a) -> p e a", e=2), rows, AX_X, ALU.max)
                link(last)
                link(nc.vector.scalar_tensor_tensor(out=neg_max[:, :, :], in0=mx[:, :, :], scalar=-SCALE,
                                                    in1=sink, op0=ALU.mult, op1=ALU.min))
                nc.vector.tensor_tensor(sink_arg[:, :, :], neg_max[:, :, :], sink, ALU.subtract
                                        ).then_inc(max_made, 1)

            def normalise(g, half):
                dve.wait_ge(exp_made, g * 2 + (half + 1))
                link(nc.vector.tensor_tensor(den[:, :, :], p_sum[:, :, :], sink_exp[:, :, :], ALU.add))
                link(nc.vector.reciprocal(r_den[:, :, :], den[:, :, :]))
                for i in range(2):
                    nk, _ = keys(2 * half + i)
                    p = probs[half][:, i, :].rearrange("p (m n) -> p m n", m=PAIRED)[:, :, 0:nk]
                    last = nc.vector.tensor_tensor(p, p, r_den[:, i, :].unsqueeze(2).to_broadcast([P, PAIRED, nk]),
                                                   ALU.mult)
                last.then_inc(probs_made, 1)

            def split_o(g, half):
                dve.wait_ge(o_hi, g * 2 + (half + 1))
                for i in range(2):
                    c = 2 * half + i
                    at = (slice(None), bass.ds(g * PAIRED, PAIRED), slice(c * CHUNK, (c + 1) * CHUNK))
                    last = nc.vector.tensor_tensor(b_lo[at], ob[i][:, 0:256].rearrange("p (h n) -> p h n", h=PAIRED),
                                                   b_hi[at].bitcast(F32), ALU.subtract)
                last.then_inc(o_lo, 1)

            LINKS = 2 * 4 + TOK

            def attend(blk, g, evac):
                copy_cur(g)
                split_next(blk, 0)
                copy_qT(g)
                row_max(g, 0)
                split_next(blk, 1)
                normalise(g, 0)
                row_max(g, 1)
                split_next(blk, 2, 3)
                normalise(g, 1)
                split_next(blk, 4)
                split_o(g, 0)
                split_next(blk, 5, 6, 7)
                if evac:
                    rotate_q(blk, 0)
                split_o(g, 1)
                if evac:
                    rotate_q(blk, 1)

            dve.wait_ge(kt_copied, 2)
            with chain.loop(0, KVH - 1, LINKS) as g:
                attend(g + (B_Q + 1), g, True)
            attend(B_WO, KVH - 1, False)
            to_y(B_WO, 0, False)
            dve.wait_ge(row_landed[0], 16)
            for t in range(TOK):
                scale_y(0, t, 0)
            finish_y(B_WO, False, 0, (UNITS, 2))
            mlp(B_MLP0, 0, UNITS, 2 * NB, (T_V, 4))

            first_block(B_V, T_V, 4)

            def v_stats(j):
                for t in range(TOK):
                    dve.wait_ge(acc_free, j * 2 + (2 * B_V + t + 1))
                    nc.vector.bn_stats(stats[:, t, bass.ds(j, 1), :].rearrange("p a n -> p (a n)"),
                                       y[:, t, bass.ds(j * COL, COL)]).then_inc(dve_chain, 1)
                    chain.n = chain.n + 1

            v_stats(0)
            with chain.loop(1, NB, TOK) as j:
                for pair in range(PAIRS):
                    split_ahead(j + B_V, pair)
                v_stats(j)
            dve.wait_ge(dve_chain, chain.n)
            for t in range(TOK):
                last = nc.vector.bn_aggr(moments[:, t, :], stats[:, t].rearrange("p j n -> p (j n)"))
            link(last)
            norms[0] += 1
            nc.vector.tensor_scalar(mean_sq[:, :], moments[:, :, 1], EPS, None, ALU.add).then_inc(norm_mean, 1)
            split_ahead(B_U, 0)
            inverse(r_out)
            dve.wait_ge(norm_done, norms[0])
            dve.wait_ge(row_landed[2], 16)
            dve.wait_ge(row_landed[3], 16)

            def layer_norm(c):
                f = slice(c * COL, (c + 1) * COL)
                for t in range(TOK):
                    last = nc.vector.scalar_tensor_tensor(out=y[:, t, f], in0=y[:, t, f], scalar=moments[:, t, 0:1],
                                                          in1=gain[:, f], op0=ALU.subtract, op1=ALU.mult)
                link(last)
                for t in range(TOK):
                    nc.vector.scalar_tensor_tensor(out=y[:, t, f], in0=y[:, t, f], scalar=r_out[:, t:t + 1],
                                                   in1=lnb[:, f], op0=ALU.mult, op1=ALU.add).then_inc(normed, 1)

            def gates_to_y(c):
                for t in range(TOK):
                    dve.wait_ge(gates_made, 2 * c + t + 1)
                    for i in range(2):
                        g = 2 * c + i
                        last = nc.vector.tensor_scalar(y[:, t, g * SGD:(g + 1) * SGD], sc[t][:, i * SGD:(i + 1) * SGD],
                                                       bs_cols[:, g:g + 1], None, ALU.add)
                    last.then_inc(gates_ready, 1)

            def apply_gates(j):
                for t in range(TOK):
                    dve.wait_ge(acc_free, j * 2 + (2 * B_U + t + 1))
                    nc.vector.tensor_tensor(s[:, t, :], s[:, t, :], y[:, t, bass.ds(j * COL, COL)], ALU.mult
                                            ).then_inc(gated, 1)

            layer_norm(0)
            for pair in range(1, PAIRS):
                split_ahead(B_U, pair)
                layer_norm(pair)
                gates_to_y(pair - 1)
            gates_to_y(3)
            dve.wait_ge(gates_ready, 2 * NB)
            apply_gates(0)
            with dve.Fori(1, NB) as j:
                split_ahead(j + B_U, 0)
                for t in range(TOK):
                    split_s(t, (j - 1) * 2 + (T_U + t), (j - 1) * 4)
                for pair in range(1, PAIRS):
                    split_ahead(j + B_U, pair)
                apply_gates(j)
            split_ahead(B_OUT, 0)
            for t in range(TOK):
                split_s(t, 2 * (NB - 1) + T_U + t, 4 * (NB - 1))
            for pair in range(1, PAIRS):
                split_ahead(B_OUT, pair)
            to_y(B_OUT, 0, False)
            dve.wait_ge(row_landed[4], 16)
            for t in range(TOK):
                scale_y(0, t, 4 * NB)
            finish_y(B_OUT, False, 4 * NB, (T_MLP1 - UNITS, 6))
            mlp(B_MLP1, 1, T_MLP1 - UNITS, 6 * NB, None)


INS = ("x", "positions", "norm_gains", "attn_w_qkv", "attn_w_o", "attn_sinks", "sgu_w_in", "sgu_ln_g", "sgu_ln_b",
       "sgu_w_s", "sgu_b_s", "sgu_w_out", "mlp_w_up", "mlp_w_down")


def kernel(**inputs):
    import concourse.bacc as bacc
    from concourse.bass_utils import run_bass_kernel_spmd

    nc = bacc.Bacc("TRN2", target_bir_lowering=False, num_devices=1)
    arrays, args = {}, []
    for name in INS:
        a = np.ascontiguousarray(inputs[name])
        arrays[f"in_{name}"] = a
        args.append(nc.dram_tensor(f"in_{name}", a.shape, mybir.dt.from_np(a.dtype), kind="ExternalInput").ap())
    out = nc.dram_tensor("out_0", arrays["in_x"].shape, F32, kind="ExternalOutput").ap()
    trunk(nc, *args, out)
    r = run_bass_kernel_spmd(nc, [arrays], core_ids=[0])
    return r.results[0]["out_0"]
```
